# Optimizing a Trainium2 kernel written in Bass

```python
import jax, jax.numpy as jnp
from jax import lax
import numpy as np
import math
import jax
import jax.numpy as jnp

D_MODEL = 1024
BATCH = 1
SEQ = 256
DEPTH = 2

POOL_WINDOWS = (2, 4, 8, 16)
POOL_GROUP = 128
POOL_WIDTH = POOL_GROUP * len(POOL_WINDOWS)
ATTN_HEADS = 8
HEAD_DIM = 64
ATTN_WIDTH = ATTN_HEADS * HEAD_DIM
MOBA_BLOCK = 256
MOBA_TOPK = 3
Q_CHUNK = 64
RNN_BLOCKS = 10
RNN_BLOCK = 128
RNN_WIDTH = RNN_BLOCKS * RNN_BLOCK
RNN_CONV = 4
RG_C = 8.0
D_FF = 2816
FFN_CONV = 3
EPS = 1e-6
NEG_INF = -1e30
N_EVEN = (DEPTH + 1) // 2
N_ODD = DEPTH // 2


def rms_norm(x, g):
    x32 = x.astype(jnp.float32)
    y = x32 * lax.rsqrt(jnp.mean(x32 * x32, axis=-1, keepdims=True) + EPS)
    return (y * g.astype(jnp.float32)).astype(x.dtype)

def causal_dwconv(x, w, b):
    K, C = w.shape
    y = lax.conv_general_dilated(
        x, w[:, None, :].astype(x.dtype), window_strides=(1,), padding=[(K - 1, 0)],
        dimension_numbers=('NWC', 'WIO', 'NWC'), feature_group_count=C)
    return y + b.astype(x.dtype)

def multiscale_pool_minus_identity(u):
    S = u.shape[1]
    u32 = u.astype(jnp.float32)
    cs = jnp.cumsum(u32, axis=1)
    count = jnp.arange(1, S + 1, dtype=jnp.float32)[None, :, None]
    outs = []
    for gi, w in enumerate(POOL_WINDOWS):
        sl = slice(gi * POOL_GROUP, (gi + 1) * POOL_GROUP)
        c = cs[..., sl]
        prev = jnp.pad(c, ((0, 0), (w, 0), (0, 0)))[:, :S]
        outs.append((c - prev) / jnp.minimum(count, float(w)) - u32[..., sl])
    return jnp.concatenate(outs, axis=-1)

def head_rms(t, g):
    t32 = t.astype(jnp.float32)
    return t32 * lax.rsqrt(jnp.mean(t32 * t32, axis=-1, keepdims=True) + EPS) * g.astype(jnp.float32)

def moba_attention(q, k, v, q_gain, k_gain):
    B, S, H, Dh = q.shape
    nb = -(-S // MOBA_BLOCK)
    s_pad = nb * MOBA_BLOCK
    pad = ((0, 0), (0, s_pad - S), (0, 0), (0, 0))
    qn = jnp.pad(head_rms(q, q_gain), pad).transpose(0, 2, 1, 3)
    kn = jnp.pad(head_rms(k, k_gain), pad).transpose(0, 2, 1, 3)
    vp = jnp.pad(v.astype(jnp.float32), pad).transpose(0, 2, 1, 3)
    k_blocks = kn.reshape(B, H, nb, MOBA_BLOCK, Dh)
    v_blocks = vp.reshape(B, H, nb, MOBA_BLOCK, Dh)
    slopes = 2.0 ** (-8.0 * jnp.arange(1, H + 1, dtype=jnp.float32) / H)
    scale = Dh ** -0.5
    topk = min(MOBA_TOPK, nb - 1)
    q_blk = jnp.arange(s_pad) // MOBA_BLOCK
    if topk > 0:
        k_mean = jnp.mean(k_blocks, axis=3)
        gate = jnp.einsum('bhqd,bhnd->bhqn', qn, k_mean)
        past = jnp.arange(nb)[None, :] < q_blk[:, None]
        gate = jnp.where(past[None, None], gate, -jnp.inf)
        _, sel_idx = lax.top_k(gate, topk)
        sel_valid = sel_idx < q_blk[None, None, :, None]
    bi = jnp.arange(B)[:, None, None, None]
    hi = jnp.arange(H)[None, :, None, None]
    kpos = jnp.arange(MOBA_BLOCK)

    def chunk(c):
        start = c * Q_CHUNK
        q_c = lax.dynamic_slice_in_dim(qn, start, Q_CHUNK, axis=2)
        t_c = start + jnp.arange(Q_CHUNK)
        own = start // MOBA_BLOCK
        k_own = lax.dynamic_index_in_dim(k_blocks, own, axis=2, keepdims=False)
        v_own = lax.dynamic_index_in_dim(v_blocks, own, axis=2, keepdims=False)
        dist_own = (t_c[:, None] - (own * MOBA_BLOCK + kpos)[None, :]).astype(jnp.float32)
        logit_own = (jnp.einsum('bhqd,bhkd->bhqk', q_c, k_own) * scale
                     - slopes[None, :, None, None] * dist_own[None, None])
        logit_own = jnp.where((dist_own >= 0)[None, None], logit_own, NEG_INF)
        if topk == 0:
            p_own = jax.nn.softmax(logit_own, axis=-1)
            return jnp.einsum('bhqk,bhkd->bhqd', p_own, v_own)
        idx_c = lax.dynamic_slice_in_dim(sel_idx, start, Q_CHUNK, axis=2)
        valid_c = lax.dynamic_slice_in_dim(sel_valid, start, Q_CHUNK, axis=2)
        k_sel = k_blocks[bi, hi, idx_c]
        v_sel = v_blocks[bi, hi, idx_c]
        s_pos = idx_c[..., None] * MOBA_BLOCK + kpos
        dist_sel = (t_c[None, None, :, None, None] - s_pos).astype(jnp.float32)
        logit_sel = (jnp.einsum('bhqd,bhqjkd->bhqjk', q_c, k_sel) * scale
                     - slopes[None, :, None, None, None] * dist_sel)
        logit_sel = jnp.where(valid_c[..., None], logit_sel, NEG_INF)
        n_sel = topk * MOBA_BLOCK
        logits = jnp.concatenate([logit_sel.reshape(B, H, Q_CHUNK, n_sel), logit_own], axis=-1)
        p = jax.nn.softmax(logits, axis=-1)
        p_sel = p[..., :n_sel].reshape(B, H, Q_CHUNK, topk, MOBA_BLOCK)
        p_own = p[..., n_sel:]
        return (jnp.einsum('bhqjk,bhqjkd->bhqd', p_sel, v_sel)
                + jnp.einsum('bhqk,bhkd->bhqd', p_own, v_own))

    outs = lax.map(chunk, jnp.arange(s_pad // Q_CHUNK))
    out = outs.transpose(1, 0, 3, 2, 4).reshape(B, s_pad, H * Dh)
    return out[:, :S]

def pool_attn_mixer(h, w_in, pool_w, pool_scale, q_gain, k_gain, w_out):
    B, S, _ = h.shape
    z = h @ w_in
    u, q, k, v = jnp.split(z, [POOL_WIDTH, POOL_WIDTH + ATTN_WIDTH, POOL_WIDTH + 2 * ATTN_WIDTH], axis=-1)
    p = multiscale_pool_minus_identity(u).astype(h.dtype)
    p = jnp.einsum('bsgc,gcd->bsgd', p.reshape(B, S, len(POOL_WINDOWS), POOL_GROUP), pool_w)
    p = p.reshape(B, S, POOL_WIDTH) * pool_scale
    a = moba_attention(q.reshape(B, S, ATTN_HEADS, HEAD_DIM), k.reshape(B, S, ATTN_HEADS, HEAD_DIM),
                       v.reshape(B, S, ATTN_HEADS, HEAD_DIM), q_gain, k_gain)
    return jnp.concatenate([p, a.astype(h.dtype)], axis=-1) @ w_out

def rglru_mixer(h, w_in, conv_w, conv_b, w_a, b_a, w_x, b_x, lam, w_out):
    B, S, _ = h.shape
    z = h @ w_in
    gate, xr = jnp.split(z, 2, axis=-1)
    xr = causal_dwconv(xr, conv_w, conv_b)
    xb = xr.reshape(B, S, RNN_BLOCKS, RNN_BLOCK)
    r = jax.nn.sigmoid((jnp.einsum('bsnc,ncd->bsnd', xb, w_a).reshape(B, S, RNN_WIDTH) + b_a).astype(jnp.float32))
    i = jax.nn.sigmoid((jnp.einsum('bsnc,ncd->bsnd', xb, w_x).reshape(B, S, RNN_WIDTH) + b_x).astype(jnp.float32))
    log_a = -RG_C * r * jax.nn.softplus(-lam.astype(jnp.float32))
    a = jnp.exp(log_a)
    b = jnp.sqrt(-jnp.expm1(2.0 * log_a)) * (i * xr.astype(jnp.float32))

    def combine(left, right):
        a1, b1 = left
        a2, b2 = right
        return a1 * a2, a2 * b1 + b2

    _, hs = lax.associative_scan(combine, (a, b), axis=1)
    y = jax.nn.gelu(gate) * hs.astype(gate.dtype)
    return y @ w_out

def conv_ffn(h, w_in, conv_w, conv_b, w_out):
    z = causal_dwconv(h @ w_in, conv_w, conv_b)
    u, g = jnp.split(z, 2, axis=-1)
    return (jax.nn.gelu(g) * u) @ w_out

def first_inputs(seed: int = 0) -> dict:
    key = jax.random.key(seed)
    ks = jax.random.split(key, 24)
    f32 = jnp.float32
    nrm = lambda k, shape, s: jax.random.normal(k, shape, f32) * s
    u = jax.random.uniform(ks[16], (N_ODD, RNN_WIDTH), f32, minval=0.9, maxval=0.999)
    a0 = u ** (1.0 / RG_C)
    return {
        "x": nrm(ks[0], (BATCH, SEQ, D_MODEL), 1.0),
        "norm_mix": 1.0 + nrm(ks[1], (DEPTH, D_MODEL), 0.05),
        "norm_ffn": 1.0 + nrm(ks[2], (DEPTH, D_MODEL), 0.05),
        "pa_w_in": nrm(ks[3], (N_EVEN, D_MODEL, POOL_WIDTH + 3 * ATTN_WIDTH), D_MODEL ** -0.5),
        "pa_pool_w": nrm(ks[4], (N_EVEN, len(POOL_WINDOWS), POOL_GROUP, POOL_GROUP), POOL_GROUP ** -0.5),
        "pa_pool_scale": 1.0 + nrm(ks[5], (N_EVEN, POOL_WIDTH), 0.1),
        "pa_q_gain": 1.0 + nrm(ks[6], (N_EVEN, HEAD_DIM), 0.05),
        "pa_k_gain": 1.0 + nrm(ks[7], (N_EVEN, HEAD_DIM), 0.05),
        "pa_w_out": nrm(ks[8], (N_EVEN, POOL_WIDTH + ATTN_WIDTH, D_MODEL), (POOL_WIDTH + ATTN_WIDTH) ** -0.5),
        "rg_w_in": nrm(ks[9], (N_ODD, D_MODEL, 2 * RNN_WIDTH), D_MODEL ** -0.5),
        "rg_conv_w": nrm(ks[10], (N_ODD, RNN_CONV, RNN_WIDTH), RNN_CONV ** -0.5),
        "rg_conv_b": nrm(ks[11], (N_ODD, RNN_WIDTH), 0.01),
        "rg_w_a": nrm(ks[12], (N_ODD, RNN_BLOCKS, RNN_BLOCK, RNN_BLOCK), RNN_BLOCK ** -0.5),
        "rg_b_a": nrm(ks[13], (N_ODD, RNN_WIDTH), 0.01),
        "rg_w_x": nrm(ks[14], (N_ODD, RNN_BLOCKS, RNN_BLOCK, RNN_BLOCK), RNN_BLOCK ** -0.5),
        "rg_b_x": nrm(ks[15], (N_ODD, RNN_WIDTH), 0.01),
        "rg_lambda": jnp.log(a0) - jnp.log1p(-a0),
        "rg_w_out": nrm(ks[17], (N_ODD, RNN_WIDTH, D_MODEL), RNN_WIDTH ** -0.5),
        "ffn_w_in": nrm(ks[18], (DEPTH, D_MODEL, 2 * D_FF), D_MODEL ** -0.5),
        "ffn_conv_w": nrm(ks[19], (DEPTH, FFN_CONV, 2 * D_FF), FFN_CONV ** -0.5),
        "ffn_conv_b": nrm(ks[20], (DEPTH, 2 * D_FF), 0.01),
        "ffn_w_out": nrm(ks[21], (DEPTH, D_FF, D_MODEL), D_FF ** -0.5),
    }

def first_block(x, norm_mix, norm_ffn, pa_w_in, pa_pool_w, pa_pool_scale, pa_q_gain, pa_k_gain,
              pa_w_out, rg_w_in, rg_conv_w, rg_conv_b, rg_w_a, rg_b_a, rg_w_x, rg_b_x, rg_lambda,
              rg_w_out, ffn_w_in, ffn_conv_w, ffn_conv_b, ffn_w_out):
    for l in range(DEPTH):
        j = l // 2
        h = rms_norm(x, norm_mix[l])
        if l % 2 == 0:
            x = x + pool_attn_mixer(h, pa_w_in[j], pa_pool_w[j], pa_pool_scale[j],
                                    pa_q_gain[j], pa_k_gain[j], pa_w_out[j])
        else:
            x = x + rglru_mixer(h, rg_w_in[j], rg_conv_w[j], rg_conv_b[j], rg_w_a[j], rg_b_a[j],
                                rg_w_x[j], rg_b_x[j], rg_lambda[j], rg_w_out[j])
        h = rms_norm(x, norm_ffn[l])
        x = x + conv_ffn(h, ffn_w_in[l], ffn_conv_w[l], ffn_conv_b[l], ffn_w_out[l])
    return x


PLE_DIM = 256
Q_BLOCK = 128
MLA_HEADS = 8
MLA_Q_RANK = 256
MLA_KV_RANK = 128
MLA_NOPE = 64
MLA_ROPE = 32
MLA_V = 64
ROPE_THETA = 10000.0
DIFF_HEADS = 4
DIFF_QK = 64
DIFF_V = 128
WIN_HEADS = 8
WIN_KV_HEADS = 2
WIN_GROUP = WIN_HEADS // WIN_KV_HEADS
WIN_HEAD_DIM = 64
WINDOW = 128
N_ALIBI = DIFF_HEADS + WIN_HEADS
N_BRANCH = 3
BRANCH_WIDTH = 512
CONV_WIDTH = 3
IN_SPLITS = (MLA_Q_RANK, MLA_KV_RANK, MLA_ROPE,
             2 * DIFF_HEADS * DIFF_QK, 2 * DIFF_HEADS * DIFF_QK, DIFF_HEADS * DIFF_V,
             WIN_HEADS * WIN_HEAD_DIM, WIN_KV_HEADS * WIN_HEAD_DIM, WIN_KV_HEADS * WIN_HEAD_DIM,
             N_BRANCH * D_MODEL)
IN_COLS = sum(IN_SPLITS)


def rms_norm_2(x, g):
    xf = x.astype(jnp.float32)
    y = xf * lax.rsqrt(jnp.mean(xf * xf, axis=-1, keepdims=True) + EPS)
    return (y * g.astype(jnp.float32)).astype(x.dtype)

def rope(x, positions):
    half = x.shape[-1] // 2
    freqs = ROPE_THETA ** (-jnp.arange(half, dtype=jnp.float32) / half)
    ang = positions.astype(jnp.float32)[:, :, None, None] * freqs
    cos, sin = jnp.cos(ang), jnp.sin(ang)
    xf = x.astype(jnp.float32)
    x1, x2 = xf[..., :half], xf[..., half:]
    return jnp.concatenate([x1 * cos - x2 * sin, x2 * cos + x1 * sin], axis=-1).astype(x.dtype)

def alibi_slopes():
    return 2.0 ** (-8.0 * jnp.arange(1, N_ALIBI + 1, dtype=jnp.float32) / N_ALIBI)

def to_blocks(t):
    b, s = t.shape[:2]
    return jnp.moveaxis(t.reshape((b, s // Q_BLOCK, Q_BLOCK) + t.shape[2:]), 1, 0)

def from_blocks(t):
    t = jnp.moveaxis(t, 0, 1)
    return t.reshape((t.shape[0], t.shape[1] * t.shape[2]) + t.shape[3:])

def mla_attention(q, k, v):
    scale = (MLA_NOPE + MLA_ROPE) ** -0.5

    def block(qb):
        s = jnp.einsum('bqhd,bkhd->bhqk', qb, k, preferred_element_type=jnp.float32) * scale
        p = jax.nn.softmax(s, axis=-1).astype(v.dtype)
        return jnp.einsum('bhqk,bkhd->bqhd', p, v)

    return from_blocks(lax.map(block, to_blocks(q)))

def diff_attention(q, k, v, positions, lam, slopes):
    scale = DIFF_QK ** -0.5
    pos_f = positions.astype(jnp.float32)

    def block(args):
        qb, pb = args
        s = jnp.einsum('bqmhd,bkmhd->bmhqk', qb, k, preferred_element_type=jnp.float32) * scale
        dist = jnp.abs(pb[:, :, None] - pos_f[:, None, :])
        s = s - slopes[None, None, :, None, None] * dist[:, None, None]
        p = jax.nn.softmax(s, axis=-1)
        a = p[:, 0] - lam * p[:, 1]
        return jnp.einsum('bhqk,bkhd->bqhd', a.astype(v.dtype), v)

    return from_blocks(lax.map(block, (to_blocks(q), to_blocks(pos_f))))

def window_attention(q, k, v, positions, sink, slopes):
    b, s_len = q.shape[:2]
    nb = s_len // Q_BLOCK
    span = Q_BLOCK + 2 * WINDOW
    scale = WIN_HEAD_DIM ** -0.5
    pad = ((0, 0), (WINDOW, WINDOW), (0, 0), (0, 0))
    kp, vp = jnp.pad(k, pad), jnp.pad(v, pad)
    pos_f = positions.astype(jnp.float32)
    posp = jnp.pad(pos_f, ((0, 0), (WINDOW, WINDOW)))
    q_local = jnp.arange(Q_BLOCK)
    k_local = jnp.arange(span)
    band = jnp.abs(k_local[None, :] - WINDOW - q_local[:, None]) <= WINDOW
    qg = q.reshape(b, s_len, WIN_KV_HEADS, WIN_GROUP, WIN_HEAD_DIM)
    slope_hg = slopes.reshape(WIN_KV_HEADS, WIN_GROUP)[None, :, :, None, None]
    sink_hg = sink.astype(jnp.float32).reshape(WIN_KV_HEADS, WIN_GROUP)[None, :, :, None, None]

    def block(args):
        n, qb, pb = args
        start = n * Q_BLOCK
        kb = lax.dynamic_slice_in_dim(kp, start, span, axis=1)
        vb = lax.dynamic_slice_in_dim(vp, start, span, axis=1)
        pk = lax.dynamic_slice_in_dim(posp, start, span, axis=1)
        key_idx = start - WINDOW + k_local
        valid = band & ((key_idx >= 0) & (key_idx < s_len))[None, :]
        s = jnp.einsum('bqhgd,bkhd->bhgqk', qb, kb, preferred_element_type=jnp.float32) * scale
        dist = jnp.abs(pb[:, :, None] - pk[:, None, :])
        s = s - slope_hg * dist[:, None, None]
        s = jnp.where(valid, s, -jnp.inf)
        m = jnp.maximum(jnp.max(s, axis=-1, keepdims=True), sink_hg)
        e = jnp.exp(s - m)
        p = e / (jnp.sum(e, axis=-1, keepdims=True) + jnp.exp(sink_hg - m))
        return jnp.einsum('bhgqk,bkhd->bqhgd', p.astype(v.dtype), vb)

    out = from_blocks(lax.map(block, (jnp.arange(nb), to_blocks(qg), to_blocks(pos_f))))
    return out.reshape(b, s_len, WIN_HEADS * WIN_HEAD_DIM)

def depthwise_conv(a, w, bias):
    out = lax.conv_general_dilated(
        a, w[:, None, :].astype(a.dtype), window_strides=(1,),
        padding=((CONV_WIDTH // 2, CONV_WIDTH // 2),),
        dimension_numbers=('NWC', 'WIO', 'NWC'), feature_group_count=a.shape[-1])
    return out + bias.astype(a.dtype)

def hybrid_layer(x, pe, positions, layer_idx, g_mix, w_in, g_q_lora, w_uq, g_kv_lora, w_ukv,
                 g_mla_q, g_mla_k, g_diff_q, g_diff_k, lam_q1, lam_k1, lam_q2, lam_k2, g_diff_out,
                 g_win_q, g_win_k, win_sink, w_branch, w_out, g_ffn, w_ffn_gate, w_ffn_up,
                 conv_w, conv_b, w_ffn_down, w_ple_proj, g_ple, g_ple_in, w_ple_gate):
    b, s, _ = x.shape
    slopes = alibi_slopes()
    h = rms_norm_2(x, g_mix)
    proj = h @ w_in
    offs = np.cumsum(IN_SPLITS)[:-1].tolist()
    c_q, c_kv, k_r, d_q, d_k, d_v, s_q, s_k, s_v, gate_logits = jnp.split(proj, offs, axis=-1)

    q = (rms_norm_2(c_q, g_q_lora) @ w_uq).reshape(b, s, MLA_HEADS, MLA_NOPE + MLA_ROPE)
    kv = (rms_norm_2(c_kv, g_kv_lora) @ w_ukv).reshape(b, s, MLA_HEADS, MLA_NOPE + MLA_V)
    k_nope, v_mla = kv[..., :MLA_NOPE], kv[..., MLA_NOPE:]
    k_rope = jnp.broadcast_to(k_r[:, :, None, :], (b, s, MLA_HEADS, MLA_ROPE))
    k = rms_norm_2(jnp.concatenate([k_nope, k_rope], axis=-1), g_mla_k)
    q = rms_norm_2(q, g_mla_q)
    q = jnp.concatenate([q[..., :MLA_NOPE], rope(q[..., MLA_NOPE:], positions)], axis=-1)
    k = jnp.concatenate([k[..., :MLA_NOPE], rope(k[..., MLA_NOPE:], positions)], axis=-1)
    o_mla = mla_attention(q, k, v_mla).reshape(b, s, BRANCH_WIDTH)

    dq = rms_norm_2(d_q.reshape(b, s, 2, DIFF_HEADS, DIFF_QK), g_diff_q)
    dk = rms_norm_2(d_k.reshape(b, s, 2, DIFF_HEADS, DIFF_QK), g_diff_k)
    dv = d_v.reshape(b, s, DIFF_HEADS, DIFF_V)
    lam_init = 0.8 - 0.6 * math.exp(-0.3 * layer_idx)
    lam = (jnp.exp(jnp.sum(lam_q1.astype(jnp.float32) * lam_k1.astype(jnp.float32)))
           - jnp.exp(jnp.sum(lam_q2.astype(jnp.float32) * lam_k2.astype(jnp.float32))) + lam_init)
    od = diff_attention(dq, dk, dv, positions, lam, slopes[WIN_HEADS:])
    o_diff = (rms_norm_2(od, g_diff_out) * (1.0 - lam_init)).reshape(b, s, BRANCH_WIDTH)

    wq = rms_norm_2(s_q.reshape(b, s, WIN_HEADS, WIN_HEAD_DIM), g_win_q)
    wk = rms_norm_2(s_k.reshape(b, s, WIN_KV_HEADS, WIN_HEAD_DIM), g_win_k)
    wv = s_v.reshape(b, s, WIN_KV_HEADS, WIN_HEAD_DIM)
    o_win = window_attention(wq, wk, wv, positions, win_sink, slopes[:WIN_HEADS])

    gates = jax.nn.sigmoid(gate_logits.reshape(b, s, N_BRANCH, D_MODEL))
    merged = (gates[:, :, 0] * (o_mla @ w_branch[0])
              + gates[:, :, 1] * (o_diff @ w_branch[1])
              + gates[:, :, 2] * (o_win @ w_branch[2]))
    x = x + merged @ w_out

    h = rms_norm_2(x, g_ffn)
    a = depthwise_conv(h @ w_ffn_gate, conv_w, conv_b)
    x = x + (jax.nn.gelu(a) * (h @ w_ffn_up)) @ w_ffn_down

    e = rms_norm_2(pe @ w_ple_proj, g_ple)
    g = jax.nn.sigmoid(rms_norm_2(x, g_ple_in) @ w_ple_gate)
    return x + g * e

def second_inputs(seed: int = 0) -> dict:
    key = jax.random.key(seed)
    ks = iter(jax.random.split(key, 40))

    def dense(shape, fan_in):
        return jax.random.normal(next(ks), shape, jnp.float32) * fan_in ** -0.5

    def gain(n):
        return 1.0 + 0.05 * jax.random.normal(next(ks), (DEPTH, n), jnp.float32)

    def small(shape, scale):
        return scale * jax.random.normal(next(ks), shape, jnp.float32)

    x = jax.random.normal(next(ks), (BATCH, SEQ, D_MODEL), jnp.float32)
    p = jax.random.normal(next(ks), (DEPTH, BATCH, SEQ, PLE_DIM), jnp.float32)
    offset = jax.random.randint(next(ks), (BATCH, 1), 0, 1024, dtype=jnp.int32)
    positions = offset + jnp.arange(SEQ, dtype=jnp.int32)[None, :]
    return {
        'x': x,
        'p': p,
        'positions': positions,
        'g_mix': gain(D_MODEL),
        'w_in': dense((DEPTH, D_MODEL, IN_COLS), D_MODEL),
        'g_q_lora': gain(MLA_Q_RANK),
        'w_uq': dense((DEPTH, MLA_Q_RANK, MLA_HEADS * (MLA_NOPE + MLA_ROPE)), MLA_Q_RANK),
        'g_kv_lora': gain(MLA_KV_RANK),
        'w_ukv': dense((DEPTH, MLA_KV_RANK, MLA_HEADS * (MLA_NOPE + MLA_V)), MLA_KV_RANK),
        'g_mla_q': gain(MLA_NOPE + MLA_ROPE),
        'g_mla_k': gain(MLA_NOPE + MLA_ROPE),
        'g_diff_q': gain(DIFF_QK),
        'g_diff_k': gain(DIFF_QK),
        'lam_q1': small((DEPTH, DIFF_QK), 0.1),
        'lam_k1': small((DEPTH, DIFF_QK), 0.1),
        'lam_q2': small((DEPTH, DIFF_QK), 0.1),
        'lam_k2': small((DEPTH, DIFF_QK), 0.1),
        'g_diff_out': gain(DIFF_V),
        'g_win_q': gain(WIN_HEAD_DIM),
        'g_win_k': gain(WIN_HEAD_DIM),
        'win_sink': small((DEPTH, WIN_HEADS), 1.0),
        'w_branch': dense((DEPTH, N_BRANCH, BRANCH_WIDTH, D_MODEL), BRANCH_WIDTH),
        'w_out': dense((DEPTH, D_MODEL, D_MODEL), D_MODEL),
        'g_ffn': gain(D_MODEL),
        'w_ffn_gate': dense((DEPTH, D_MODEL, D_FF), D_MODEL),
        'w_ffn_up': dense((DEPTH, D_MODEL, D_FF), D_MODEL),
        'conv_w': dense((DEPTH, CONV_WIDTH, D_FF), CONV_WIDTH),
        'conv_b': small((DEPTH, D_FF), 0.02),
        'w_ffn_down': dense((DEPTH, D_FF, D_MODEL), D_FF),
        'w_ple_proj': dense((DEPTH, PLE_DIM, D_MODEL), PLE_DIM),
        'g_ple': gain(D_MODEL),
        'g_ple_in': gain(D_MODEL),
        'w_ple_gate': dense((DEPTH, D_MODEL, D_MODEL), D_MODEL),
    }

def second_block(x, p, positions, g_mix, w_in, g_q_lora, w_uq, g_kv_lora, w_ukv, g_mla_q, g_mla_k,
              g_diff_q, g_diff_k, lam_q1, lam_k1, lam_q2, lam_k2, g_diff_out, g_win_q, g_win_k,
              win_sink, w_branch, w_out, g_ffn, w_ffn_gate, w_ffn_up, conv_w, conv_b, w_ffn_down,
              w_ple_proj, g_ple, g_ple_in, w_ple_gate):
    for i in range(DEPTH):
        x = hybrid_layer(
            x, p[i], positions, i, g_mix[i], w_in[i], g_q_lora[i], w_uq[i], g_kv_lora[i], w_ukv[i],
            g_mla_q[i], g_mla_k[i], g_diff_q[i], g_diff_k[i], lam_q1[i], lam_k1[i], lam_q2[i],
            lam_k2[i], g_diff_out[i], g_win_q[i], g_win_k[i], win_sink[i], w_branch[i], w_out[i],
            g_ffn[i], w_ffn_gate[i], w_ffn_up[i], conv_w[i], conv_b[i], w_ffn_down[i],
            w_ple_proj[i], g_ple[i], g_ple_in[i], w_ple_gate[i])
    return x


def setup_inputs(seed=0):
    out = dict(first_inputs(seed))
    for name, value in second_inputs(seed + 1).items():
        if name != "x":
            out[name + "_2"] = value
    return out


def reference(
    x, norm_mix, norm_ffn, pa_w_in, pa_pool_w, pa_pool_scale, pa_q_gain, pa_k_gain, pa_w_out,
    rg_w_in, rg_conv_w, rg_conv_b, rg_w_a, rg_b_a, rg_w_x, rg_b_x, rg_lambda, rg_w_out,
    ffn_w_in, ffn_conv_w, ffn_conv_b, ffn_w_out, p_2, positions_2, g_mix_2, w_in_2, g_q_lora_2,
    w_uq_2, g_kv_lora_2, w_ukv_2, g_mla_q_2, g_mla_k_2, g_diff_q_2, g_diff_k_2, lam_q1_2,
    lam_k1_2, lam_q2_2, lam_k2_2, g_diff_out_2, g_win_q_2, g_win_k_2, win_sink_2, w_branch_2,
    w_out_2, g_ffn_2, w_ffn_gate_2, w_ffn_up_2, conv_w_2, conv_b_2, w_ffn_down_2, w_ple_proj_2,
    g_ple_2, g_ple_in_2, w_ple_gate_2,
):
    x = first_block(
        x, norm_mix, norm_ffn, pa_w_in, pa_pool_w, pa_pool_scale, pa_q_gain, pa_k_gain,
        pa_w_out, rg_w_in, rg_conv_w, rg_conv_b, rg_w_a, rg_b_a, rg_w_x, rg_b_x, rg_lambda,
        rg_w_out, ffn_w_in, ffn_conv_w, ffn_conv_b, ffn_w_out,
    )
    return second_block(
        x, p_2, positions_2, g_mix_2, w_in_2, g_q_lora_2, w_uq_2, g_kv_lora_2, w_ukv_2,
        g_mla_q_2, g_mla_k_2, g_diff_q_2, g_diff_k_2, lam_q1_2, lam_k1_2, lam_q2_2, lam_k2_2,
        g_diff_out_2, g_win_q_2, g_win_k_2, win_sink_2, w_branch_2, w_out_2, g_ffn_2,
        w_ffn_gate_2, w_ffn_up_2, conv_w_2, conv_b_2, w_ffn_down_2, w_ple_proj_2, g_ple_2,
        g_ple_in_2, w_ple_gate_2,
    )


_drawn_inputs = setup_inputs


def setup_inputs(seed=0):
    import zlib

    import numpy as np

    out = dict(_drawn_inputs(seed))
    spreads = {}
    factors = {'pa_q_gain': 4.505,
     'pa_k_gain': 4.939,
     'rg_b_a': 8.0,
     'rg_b_x': 8.0,
     'ffn_conv_b': 3.988,
     'g_q_lora_2': 8.0,
     'g_kv_lora_2': 8.0,
     'g_mla_q_2': 8.0,
     'g_mla_k_2': 8.0,
     'g_diff_q_2': 3.311,
     'g_diff_k_2': 3.445,
     'lam_q1_2': 9.197,
     'lam_q2_2': 8.0,
     'lam_k2_2': 5.05,
     'g_diff_out_2': 3.131,
     'g_win_q_2': 8.0,
     'g_win_k_2': 8.0,
     'conv_b_2': 5.702,
     'g_ple_2': 2.692,
     'g_ple_in_2': 7.198}
    for name, (base, spread) in spreads.items():
        noise = np.random.default_rng([zlib.crc32(name.encode()), seed]).standard_normal(out[name].shape)
        drawn = base * np.exp(spread * noise) if base else spread * noise
        out[name] = jnp.asarray(drawn.astype(out[name].dtype))
    for name, factor in factors.items():
        out[name] = (out[name] * factor).astype(out[name].dtype)
    return out
```

```python
from contextlib import ExitStack

import concourse.bass as bass
from concourse import mybir

ALU = mybir.AluOpType
ACT = mybir.ActivationFunctionType
AX = mybir.AxisListType
F32 = mybir.dt.float32
F32R = mybir.dt.float32r
I32 = mybir.dt.int32

P = 128
S = 256
D = 1024
DT = D // P
UW = 2048
EPS = 1e-6
TWO_PI = 6.283185307179586
TWO_PI_PARTS = (6.28125, 0.0019350051879882812, 3.0199157663e-07)
ROUND = 1.5 * 2.0 ** 23
PI_LOW = 3.1415925
LAM0 = (0.8 - 0.6 * 2.718281828459045 ** (-0.3 * 0), 0.8 - 0.6 * 2.718281828459045 ** (-0.3 * 1))
NRAW, NW = 2, 3

FF_STEPS = 11
LOOPED = 6
RG_STEPS = 5

STAGES = ("pa", "ffn0", "rg", "ffn1", "hy0", "hf0", "ple0", "hy1", "hf1", "ple1")
UNITS = {"pa": 12, "ffn": 33, "rg": 15, "hy": 35, "hf": 33, "ple": 5}
GAIN = {"pa": "norm_mix0", "ffn0": "norm_ffn0", "rg": "norm_mix1", "ffn1": "norm_ffn1", "hy0": "g_mix0", "hf0": "g_ffn0",
        "ple0": "g_ple_in0", "hy1": "g_mix1", "hf1": "g_ffn1", "ple1": "g_ple_in1"}
SCALED = {"pa": 6, "ffn": 2 * FF_STEPS, "rg": 2 * RG_STEPS, "hy": 21, "hf": 2 * FF_STEPS, "ple": 4}


def kind(stage):
    return stage.rstrip("01") if stage != "pa" else "pa"


def unit_bases():
    at, out = 0, {}
    for st in STAGES:
        out[st] = at
        at += UNITS[kind(st)]
    return out, at


CONSTS = [("ident", P), ("ones", P), ("perm", P), ("pick", 32), ("rpick", 32), ("kpick", 16), ("spread", 8 * P),
          ("rspread", 4 * P), ("win_mask", 2 * S), ("freq", 1), ("scale_pair", 3)]
VECS = [("norm_mix0", 8), ("norm_ffn0", 8), ("norm_mix1", 8), ("norm_ffn1", 8), ("pool_scale", 4), ("pa_gain", 8),
        ("cf0", FF_STEPS * 16), ("cf1", FF_STEPS * 16), ("rgv", RG_STEPS * 16)] + [
    (f"{n}{L}", w) for L in range(2) for n, w in (
        ("g_mix", 8), ("g_ffn", 8), ("g_ple", 8), ("g_ple_in", 8), ("g_cq", 2), ("g_ckv", 1), ("g_diff", 8),
        ("g_win", 5), ("g_mla", 10), ("g_krope", 1), ("g_dout", 1), ("sink", 8), ("cg", FF_STEPS * 8))]


def columns(table):
    at, out = 0, {}
    for name, w in table:
        out[name] = (at, w)
        at += w
    return out, at


def build(nc, W, XT, CON, CON0, VEC, PW, RW, PE_T, POSR, POSC, LAM, OUT, stages=STAGES):
    con_at, con_w = columns(CONSTS)
    vec_at, vec_w = columns(VECS)
    base, n_units = unit_bases()

    with ExitStack() as ctx:
        def sb(name, shape, dt=F32):
            return ctx.enter_context(nc.sbuf_tensor(name, shape, dt))

        def sem(name):
            return ctx.enter_context(nc.semaphore(name))

        bank = [ctx.enter_context(nc.psum_tensor(f"bank{i}", [P, 512], F32)) for i in range(8)]

        raw = sb("raw", [P, NRAW, UW])
        w_hi = sb("w_hi", [P, NW, UW], F32R)
        w_lo = sb("w_lo", [P, NW, UW], F32R)
        x = sb("x", [P, DT, S])
        hf = sb("hf", [P, DT, S])
        h_hi = sb("h_hi", [P, DT, S], F32R)
        h_lo = sb("h_lo", [P, DT, S], F32R)
        sq = sb("sq", [P, DT, S])
        crs = sb("crs", [P, 3, S])
        rinv_t = sb("rinv_t", [P, S + 2])
        rinv = rinv_t[:, 0:S]
        y_hi = sb("y_hi", [P, 2, 2, S], F32R)
        y_lo = sb("y_lo", [P, 2, 2, S], F32R)
        con = sb("con", [P, con_w])
        vec = sb("vec", [P, vec_w])
        wide = sb("wide", [P, 24, S])
        qk = sb("qk", [P, 25, S])
        val = sb("val", [P, 9 * S])
        lg = sb("lg", [P, 2, 512])
        pt = sb("pt", [P, 2, 512])
        ot = sb("ot", [P, 2, 512])
        geo = sb("geo", [P, 4, S])
        hr_t = sb("hr_t", [P, S])
        hr = hr_t[0:16, :]
        eps_t = sb("eps_t", [P, 1])
        eps = eps_t[:, 0:1]
        nm = sb("nm", [P, 24, 2])
        sums = sb("sums", [P, 24, 2])
        esink = sb("esink", [P, 8, 2])
        nsink = sb("nsink", [P, 8])
        rec = sb("rec", [P, 4, 2])
        dtmp = crs[:, 0].rearrange("p (a n) -> p a n", a=2)
        odss = sb("odss", [P, 4, 2])
        odr = sb("odr", [P, 4, 2])
        posr = sb("posr", [P, S], I32)
        posc = sb("posc", [P, 2], I32)
        posf, half_sin = lg[:, 1, 0:S], lg[:, 1, S:2 * S]
        poscf = sb("poscf", [P, 2])
        lamv = sb("lamv", [P, 512])
        lamp = lg[:, 0, 0:128].rearrange("p (a n) -> p a n", a=2)
        lamt = sb("lamt", [P, 5])
        rgt = wide[:, 15, 0:60].rearrange("p (a n) -> p a n", a=6)
        cpos = sb("cpos", [P, 10])
        cneg = sb("cneg", [P, 10])
        lamr = vec[:, vec_at["rgv"][0] + 7:vec_at["rgv"][0] + 16 * RG_STEPS:8]
        flat = wide[:].rearrange("p a n -> p (a n)")
        pa_con = flat[:, 15 * S:21 * S]
        pool_u, pool_a, pool_b = (flat[:, j * 4 * (S + 8):(j + 1) * 4 * (S + 8)].rearrange("p (a n) -> p a n", a=4)
                                  for j in range(3))

        def c_(name):
            a, w = con_at[name]
            return con[:, a:a + w]

        def v_(name, j=0, w=1):
            a, _ = vec_at[name]
            return vec[:, a + j:a + j + w]

        def pair(t, j):
            return t[:, 2 * j:2 * j + 2, :].rearrange("p a n -> p (a n)")

        names = """con_in x_in vec_in pos_in pa_in pool_in rg_in pe_in out_done
            setup geo_trig geo_ready lam_exp rgc_act rgc_ready
            hi_done lo_done w_used
            x_up sq_ready st_done rms_done rinv_done hhi_done h_ready scaled
            acc_done br_up mg_up ple_ev h2hi h2_ready
            grp_done in_ev hst_mm krsq hroot hr_ready bc_done qk_done
            cst_done crms cf_done chi c_ready rope_mm rope_done kro_done
            s_done lp_done exp_done pt_done pt_ev pv_done o_ev od_free od_ss od_root
            pool_p pm_done psc sig_done bhi b_ready
            tu tg cvu cvg gelu ymul yhi ffy
            rgelu rtx xcv rmm rsig rth rm rsb rgy ryhi ry_ready
            est_done erms pehi pe_ready
            act_chain dve_chain pool_chain""".split()
        sems = {n: sem(n) for n in names}
        raw_in = [sem(f"raw_in{i}") for i in range(NRAW)]

        def plus(c, i, k):
            return c if i is None else i * k + c

        class Chain:
            def __init__(self, eng, s):
                self.eng, self.s, self.n, self.i, self.k = eng, sems[s], 0, None, 0

            def __call__(self, ins):
                self.n += 1
                ins.then_inc(self.s, 1)
                self.eng.wait_ge(self.s, plus(self.n, self.i, self.k))

            def enter(self, i, k):
                self.i, self.k, self.n0 = i, k, self.n

            def leave(self, count):
                assert self.n - self.n0 == self.k, (self.n - self.n0, self.k)
                self.n = self.n0 + self.k * count
                self.i = None

        used = [s for s in STAGES if s in stages]
        first = base[used[0]]
        B = {s: base[s] - first for s in used}
        N_UNITS = min(base[used[-1]] + UNITS[kind(used[-1])] - first + 3, n_units - first)
        NORM = {s: i for i, s in enumerate(used)}
        hys = [s for s in used if kind(s) == "hy"]
        atts = [s for s in used if kind(s) in ("pa", "hy")]
        ffs = [s for s in used if kind(s) in ("ffn", "hf")]
        ffs_hf = [s for s in used if kind(s) == "hf"]
        causals = [s for s in used if kind(s) == "ffn"]
        ples = [s for s in used if kind(s) == "ple"]

        def scaled_before(s):
            return sum(SCALED[kind(a)] for a in used[:used.index(s)])

        def parts_late(s, step):
            return kind(s) == "hf" or step == FF_STEPS - 1

        LAST = {"pa": [11], "ffn": [32], "rg": [14], "hf": [32], "hy": [26, 28, 30, 34], "ple": [0, 4]}
        gemms = [(s, j) for s in used for j in range(len(LAST[kind(s)]))]

        def acc_ready(eng, s, j, b):
            if b < 3:
                eng.wait_ge(sems["acc_done"], 3 * gemms.index((s, j)) + b + 1)
            else:
                eng.wait_ge(sems["w_used"], B[s] + LAST[kind(s)][j] + 1)

        def acc_free(eng, s, j, b):
            i = gemms.index((s, j))
            if i:
                ps, pj = gemms[i - 1]
                if kind(ps) == "hy" and pj < 3:
                    eng.wait_ge(sems["br_up"], 12 * hys.index(ps) + 4 * pj + b + 1)
                elif kind(ps) == "ple":
                    eng.wait_ge(sems["ple_ev"], 8 * ples.index(ps) + 4 * pj + b + 1)
                else:
                    eng.wait_ge(sems["x_up"], 4 * NORM[ps] + b + 1)

        PLAN = {
            "pa": dict(groups=8, parts=0, pairs=[4], maps=8, ogroups=2, opairs=2),
            "hy": dict(groups=30, parts=5, pairs=[4, 3, 6], maps=24, ogroups=8, opairs=6)}

        def total(s, what):
            n = 0
            for a in atts:
                if a == s:
                    break
                v = PLAN[kind(a)][what]
                n += sum(v) if isinstance(v, list) else v
            return n

        def nsets(s):
            return sum(len(PLAN[kind(a)]["pairs"]) for a in atts[:atts.index(s)])

        def group_ready(eng, s, e):
            ub = B[s]
            if kind(s) == "pa" or e <= 10:
                eng.wait_ge(sems["w_used"], ub + e + 1)
            elif e in (11, 12, 14, 15, 16):
                eng.wait_ge(sems["grp_done"], total(s, "parts") + {11: 1, 12: 2, 14: 3, 15: 4, 16: 5}[e])
            else:
                eng.wait_ge(sems["w_used"], ub + {13: 11, 17: 12}.get(e, e - 5) + 1)

        def scale_no(s, e):
            es = [0, 1, 2, 3, 6, 7] if kind(s) == "pa" else [0, 1, 2, 3, 4, 5, 8, 9, 10] + list(range(18, 30))
            return scaled_before(s) + es.index(e) + 1 if e in es else None

        def att_maps(s):
            out = []
            if kind(s) == "pa":
                for h in range(8):
                    p = 64 * (h % 2)
                    out.append(dict(q=[(h // 2, p, 64)], k=[(4 + h // 2, p, 64)], dist="causal", slope=2.0 ** -(h + 1),
                                    v=("pa", h), g=h // 4, slot=h % 4, w=64, sink=None))
                return out
            al = [2.0 ** (-8.0 * (i + 1) / 12) for i in range(12)]
            for h in range(4):
                for m in range(2):
                    t, p = 2 * m + h // 2, 64 * (h % 2)
                    out.append(dict(q=[(t, p, 64)], k=[(4 + t, p, 64)], dist="plain", slope=al[8 + h],
                                    v=("diff", h), g=h, slot=m, w=128, sink=None))
            for h in range(8):
                p = 64 * (h // 4)
                out.append(dict(q=[(8 + h % 4, p, 64)], k=[(12, p, 64)], dist="win", slope=al[h],
                                v=("win", h // 4), g=4 + h // 4, slot=h % 4, w=64, sink=h))
            for h in range(8):
                p, r = 64 * (h % 2), 32 * (h % 4)
                out.append(dict(q=[(13 + h // 2, p, 64), (17 + h // 4, r, 32)],
                                k=[(19 + h // 2, p, 64), (23 + h // 4, r, 32)], dist=None, slope=None,
                                v=("mla", h), g=6 + h // 4, slot=h % 4, w=64, sink=None))
            return out

        def value(v, kt):
            which, h = v
            o, w = {"pa": ((h // 4) * 512 + kt * 256 + (h % 4) * 64, 64),
                    "diff": ((h // 2) * 512 + kt * 256 + (h % 2) * 128, 128),
                    "mla": (1024 + kt * 512 + h * 64, 64), "win": (2048 + kt * 128 + h * 64, 64)}[which]
            return val[:, o:o + w]

        def ended(s, i):
            ms = att_maps(s)
            if i < 0 or i >= len(ms):
                return None
            return ms[i]["g"] if i + 1 == len(ms) or ms[i + 1]["g"] != ms[i]["g"] else None

        TURNS = {"pa": {5: [0], 8: [1]}, "hy": {10: [0], 11: [1], 13: [2], 17: [3], 21: [4], 24: [5]}}

        def uses(s, i):
            n = PLAN[kind(s)]["maps"]
            return ([("map", i)] if i < n else []) + [("pair", p) for p in TURNS[kind(s)].get(i, [])]

        def use_no(s, what):
            n = total(s, "maps") + total(s, "opairs")
            for i in range(PLAN[kind(s)]["maps"] + 1):
                for u in uses(s, i):
                    if u == what:
                        return n
                    n += 1

        def ot_tiles(s, p):
            if kind(s) == "pa":
                return pair(hf, 2 + p)
            return pair(hf, p) if p < 4 else pair(qk, p - 4)

        cq = ot[:].rearrange("p a (b n) -> p (a b) n", b=2)

        block = ctx.enter_context(nc.Block())

        @block.sync
        def _(sp):
            sp.dma_start(vec[:], VEC).then_inc(sems["vec_in"], 16)
            sp.dma_start(x[:], XT).then_inc(sems["x_in"], 16)
            sp.dma_start(raw[:, 0], W[first]).then_inc(raw_in[0], 16)
            sp.dma_start(con[:], CON).then_inc(sems["con_in"], 16)
            sp.dma_start(raw[:, 1], W[first + 1]).then_inc(raw_in[1], 16)
            sp.dma_start(posr[:], POSR.broadcast_to([P, S]))\
              .then_inc(sems["pos_in"], 16)
            sp.dma_start(posc[:], POSC).then_inc(sems["pos_in"], 16)
            sp.dma_start(lamv[:], LAM.broadcast_to([P, 8 * 64])).then_inc(sems["pos_in"], 16)
            if "pa" in used:
                sp.dma_start(pa_con, CON0).then_inc(sems["pa_in"], 16)
                sp.dma_start(wide[:, 13:15].rearrange("p a n -> p (a n)"), PW).then_inc(sems["pool_in"], 16)
            with sp.Fori(0, N_UNITS // 2 - 1) as i:
                for j in range(2):
                    sp.wait_ge(sems["lo_done"], i * 2 + (j + 1))
                    sp.dma_start(raw[:, j], W[bass.ds(i * 2 + (first + 2 + j), 1)].rearrange("a p n -> p (a n)"))\
                      .then_inc(raw_in[j], 16)
            if N_UNITS % 2:
                sp.wait_ge(sems["lo_done"], N_UNITS - 2)
                sp.dma_start(raw[:, 0], W[first + N_UNITS - 1]).then_inc(raw_in[0], 16)
            sp.wait_ge(sems["x_up"], 4 * len(used))
            sp.dma_start(OUT, x[:]).then_inc(sems["out_done"], 16)
            sp.wait_ge(sems["out_done"], 16)

        @block.scalar
        def _(act):
            state = {"split": 0}
            link = Chain(act, "act_chain")

            def split(n0, i=None):
                act.wait_ge(raw_in[n0 % NRAW], plus(16 * (n0 // NRAW + 1), i, 48))
                if n0 >= NW:
                    act.wait_ge(sems["w_used"], plus(n0 - NW + 1, i, 6))
                nc.scalar.activation(w_hi[:, n0 % NW], raw[:, n0 % NRAW], ACT.Copy).then_inc(sems["hi_done"], 1)

            def after(n, i=None):
                if i is None:
                    while state["split"] <= min(n + 3, N_UNITS - 1):
                        split(state["split"])
                        state["split"] += 1
                else:
                    split(n + 3, i)

            def norm(s, between=None):
                k = NORM[s]
                for j in range(4):
                    if k == 0:
                        act.wait_ge(sems["x_in"], 16)
                    else:
                        act.wait_ge(sems["x_up"], 4 * k + j - 3)
                    for t in (2 * j, 2 * j + 1):
                        last = nc.scalar.activation(h_hi[:, t], x[:, t], ACT.Copy, scale=v_(GAIN[s], t))
                    last.then_inc(sems["hhi_done"], 1)
                if k == 0:
                    after(-3)
                for j in range(4):
                    nc.scalar.activation(pair(sq, j), pair(x, j), ACT.Square).then_inc(sems["sq_ready"], 1)
                if between:
                    between()
                after(B[s] - 1)
                act.wait_ge(sems["st_done"], k + 1)
                w = S + 2 if s in atts else S
                nc.scalar.activation(rinv_t[:, 0:w], bank[6][:, 0:w], ACT.Sqrt, bias=eps, scale=1.0 / D)\
                    .then_inc(sems["rms_done"], 1)

            def ffn(s):
                f, ub, causal = ffs.index(s), B[s], kind(s) == "ffn"
                cols = f"cf{s[-1]}" if causal else f"cg{s[-1]}"
                nt, tap = (4, 2) if causal else (2, 1)
                T = qk[:, 0:4, :]
                c0 = scaled_before(s)

                def taps(t, s0, i):
                    o = vec_at[cols][0] + 4 * (nt * s0 + t)
                    if i is None:
                        return vec[:, o + tap:o + tap + 1], vec[:, o + 3:o + 4]
                    return vec[:, bass.ds(i * (8 * nt) + (o + tap), 1)], vec[:, bass.ds(i * (8 * nt) + (o + 3), 1)]

                def step(s0, i=None):
                    u = ub + (3 * s0 - 1 if s0 else 0)
                    done = lambda c: plus(FF_STEPS * f + s0 + c, i, 2)
                    late = parts_late(s, s0)
                    if not late:
                        after(u, i)
                    if f or s0:
                        act.wait_ge(sems["ymul"], done(0))
                    act.wait_ge(sems["scaled"], plus(c0 + 2 * s0 + 1, i, 4))
                    for t in range(2):
                        w, b = taps(t, s0, i)
                        ins = nc.scalar.activation(T[:, t], bank[4][:, t * S:(t + 1) * S], ACT.Identity, bias=b, scale=w)
                    ins.then_inc(sems["tu"], 1)
                    if late:
                        after(u, i)
                    elif causal:
                        after(u + 1, i)
                    if causal:
                        act.wait_ge(sems["scaled"], plus(c0 + 2 * s0 + 2, i, 4))
                        for t in range(2, 4):
                            w, b = taps(t, s0, i)
                            ins = nc.scalar.activation(T[:, t], bank[5][:, (t - 2) * S:(t - 1) * S], ACT.Identity,
                                                       bias=b, scale=w)
                        ins.then_inc(sems["tg"], 1)
                    act.wait_ge(sems["cvg"], done(1))
                    nc.scalar.activation(pair(qk, 2), pair(qk, 1 if causal else 0), ACT.Gelu_apprx_tanh)\
                        .then_inc(sems["gelu"], 1)
                    if late or not causal:
                        after(u + 1, i)
                    if s0 and not late:
                        after(u + 2, i)
                    act.wait_ge(sems["ymul"], done(1))
                    if s0:
                        act.wait_ge(sems["w_used"], plus(u + 3, i, 6))
                    nc.scalar.activation(pair(y_hi[:, 0], 0), pair(qk, 3), ACT.Copy).then_inc(sems["yhi"], 1)
                    if s0 and late:
                        after(u + 2, i)

                for s0 in range(3):
                    step(s0)
                with act.Fori(0, LOOPED // 2) as i:
                    step(3, i)
                    step(4, i)
                state["split"] = ub + 3 * (3 + LOOPED) + 2
                for s0 in range(3 + LOOPED, FF_STEPS):
                    step(s0)

            def evacuate(s, e, dst, square=None, src=slice(0, 512)):
                c = scale_no(s, e)
                if c is None:
                    group_ready(act, s, e)
                else:
                    act.wait_ge(sems["scaled"], c)
                b = bank[(total(s, "groups") + e) % 2]
                z = b[:, src]
                if len(dst.shape) == 3:
                    z = z.rearrange("p (a n) -> p a n", a=2)
                last = nc.scalar.activation(dst, z, ACT.Copy)
                if square is not None:
                    last = nc.scalar.activation(square, b[:, src], ACT.Square)
                last.then_inc(sems["in_ev"], 1)

            def token_values(s, e, o, src=0, w=256):
                group_ready(act, s, e)
                act.wait_ge(sems["rinv_done"], NORM[s] + 1)
                b = bank[(total(s, "groups") + e) % 2]
                for kt in range(2):
                    last = nc.scalar.activation(val[:, o + kt * w:o + (kt + 1) * w], b[:, src + kt * w:src + (kt + 1) * w],
                                                ACT.Copy, scale=rinv_t[:, S + kt:S + kt + 1])
                return last

            def set_slot(s, k):
                q = total(s, "pairs") + k
                if k >= 4:
                    act.wait_ge(sems["hst_mm"], q - 3)
                return pair(sq, k % 4)

            def set_root(s, j, dim):
                last = sum(PLAN[kind(s)]["pairs"][:j + 1])
                act.wait_ge(sems["hst_mm"], total(s, "pairs") + last)
                if j:
                    act.wait_ge(sems["bc_done"], total(s, "pairs") + sum(PLAN[kind(s)]["pairs"][:j]))
                nc.scalar.activation(hr, bank[6][0:16, 0:S], ACT.Sqrt, bias=eps[0:16], scale=1.0 / dim)\
                    .then_inc(sems["hroot"], 1)

            def turn(s, u):
                n = use_no(s, u)
                act.wait_ge(sems["pt_done"], n + 1)
                src = bank[6 + n % 2][:]
                if u[0] == "map":
                    nc.scalar.activation(pt[:, u[1] % 2], src, ACT.Copy).then_inc(sems["pt_ev"], 1)
                elif kind(s) == "hy" and u[1] < 2:
                    nc.scalar.activation(ot_tiles(s, u[1]), src, ACT.Copy, scale=v_(f"g_dout{s[-1]}"))\
                        .then_inc(sems["pt_ev"], 1)
                else:
                    nc.scalar.activation(ot_tiles(s, u[1]), src, ACT.Copy).then_inc(sems["pt_ev"], 1)

            def softmax(s, i):
                m, n = att_maps(s)[i], total(s, "maps") + i
                act.wait_ge(sems["lp_done"], n + 1)
                for qt in range(2):
                    p = lg[:, i % 2, qt * S:(qt + 1) * S]
                    if m["dist"]:
                        src, sc = p, -1.0
                    else:
                        src, sc = bank[4 + i % 2][:, qt * S:(qt + 1) * S], 1.0
                    if m["sink"] is not None:
                        h = m["sink"]
                        nc.scalar.activation(esink[:, h, qt:qt + 1], v_(f"sink{s[-1]}", h), ACT.Exp,
                                             bias=nm[:, i, qt:qt + 1])
                    last = nc.scalar.activation(p, src, ACT.Exp, bias=nm[:, i, qt:qt + 1], scale=sc,
                                                accum_out=sums[:, i, qt:qt + 1])
                last.then_inc(sems["exp_done"], 1)

            def branch_input(s, p):
                ub = B[s]
                act.wait_ge(sems["pt_ev"], use_no(s, ("pair", p)) + 1)
                if p >= 2:
                    act.wait_ge(sems["w_used"], ub + 25 + p - 1)
                    after(ub + 25 + p - 2)
                nc.scalar.activation(y_hi[:, p % 2].rearrange("p a n -> p (a n)"), ot_tiles(s, p), ACT.Copy)\
                    .then_inc(sems["bhi"], 1)

            def attention(s, fillers):
                n = PLAN[kind(s)]["maps"]
                for i in range(n + 1):
                    if kind(s) == "hy" and i == n - 2:
                        branch_input(s, 0)
                        branch_input(s, 1)
                    if i:
                        for u in uses(s, i - 1):
                            turn(s, u)
                    if i < n:
                        softmax(s, i)
                    if i in fillers:
                        unit, e, dst = fillers[i]
                        after(unit)
                        evacuate(s, e, dst)
                    if kind(s) == "hy" and i == 8:
                        act.wait_ge(sems["od_ss"], hys.index(s) + 1)
                        nc.scalar.activation(odr[:], odss[:], ACT.Sqrt, bias=eps, scale=1.0 / 128)\
                            .then_inc(sems["od_root"], 1)
                for u in uses(s, n):
                    turn(s, u)

            def to_h(s, src, j):
                nc.scalar.activation(pair(h_hi, j), pair(src, j), ACT.Copy).then_inc(sems["h2hi"], 1)

            def pa(s):
                ub = B[s]
                norm(s)
                for e in range(4):
                    after(ub + e)
                    evacuate(s, e, pair(qk, e), set_slot(s, e))
                for e in (4, 5):
                    after(ub + e)
                    token_values(s, e, 512 * (e - 4)).then_inc(sems["in_ev"], 1)
                    if e == 4:
                        set_root(s, 0, 64)
                attention(s, {1: (ub + 6, 6, pool_u[:, 0:2, 8:8 + S]), 3: (ub + 7, 7, pool_u[:, 2:4, 8:8 + S])})
                for j in range(2):
                    act.wait_ge(sems["pm_done"], j + 1)
                    for t in range(2):
                        last = nc.scalar.activation(hf[:, 2 * j + t], bank[j][:, t * S:(t + 1) * S], ACT.Copy,
                                                    scale=v_("pool_scale", 2 * j + t))
                    last.then_inc(sems["psc"], 1)
                    act.wait_ge(sems["psc"], j + 1)
                    to_h(s, hf, j)
                for p in range(2):
                    act.wait_ge(sems["pt_ev"], use_no(s, ("pair", p)) + 1)
                    to_h(s, hf, 2 + p)
                for n in range(8, 11):
                    after(ub + n)

            def rg(s):
                ub = B[s]
                act.dma_start(wide[:, 0:10].rearrange("p a n -> p (a n)"), RW).then_inc(sems["rg_in"], 16)
                norm(s)
                c0 = scaled_before(s)
                for k in range(RG_STEPS):
                    u = ub + (3 * k - 1 if k else 0)
                    vb = lambda t, c: v_("rgv", 16 * k + 8 * t + c)
                    after(u)
                    act.wait_ge(sems["scaled"], c0 + 2 * k + 1)
                    if k:
                        act.wait_ge(sems["rgy"], k)
                    nc.scalar.activation(pair(qk, 1), bank[4][:], ACT.Gelu_apprx_tanh).then_inc(sems["rgelu"], 1)
                    after(u + 1)
                    act.wait_ge(sems["scaled"], c0 + 2 * k + 2)
                    for t in range(2):
                        last = nc.scalar.activation(qk[:, t], bank[5][:, t * S:(t + 1) * S], ACT.Identity,
                                                    bias=vb(t, 4), scale=vb(t, 3))
                    last.then_inc(sems["rtx"], 1)
                    if k == 0:
                        link(nc.scalar.activation(rgt[:, 0], lamr, ACT.Abs))
                        nc.scalar.activation(rgt[:, 1], rgt[:, 0], ACT.Exp, scale=-1.0).then_inc(sems["rgc_act"], 1)
                        act.wait_ge(sems["rgc_act"], 1)
                        nc.scalar.activation(rgt[:, 2], rgt[:, 1], ACT.Ln, bias=1.0).then_inc(sems["rgc_act"], 1)
                    else:
                        after(u + 2)
                    act.wait_ge(sems["rmm"], k + 1)
                    for t in range(2):
                        nc.scalar.activation(qk[:, 4 + t], bank[6][:, t * S:(t + 1) * S], ACT.Sigmoid, bias=vb(t, 5))
                    for t in range(2):
                        last = nc.scalar.activation(qk[:, 6 + t], bank[7][:, t * S:(t + 1) * S], ACT.Sigmoid, bias=vb(t, 6))
                    last.then_inc(sems["rsig"], 1)
                    act.wait_ge(sems["rsig"], k + 1)
                    if k == 0:
                        act.wait_ge(sems["rgc_ready"], 1)
                    for t in range(2):
                        nc.scalar.activation(qk[:, 8 + t], qk[:, 4 + t], ACT.Tanh, scale=cpos[:, 2 * k + t:2 * k + t + 1])
                    for t in range(2):
                        last = nc.scalar.activation(qk[:, 10 + t], qk[:, 4 + t], ACT.Exp,
                                                    scale=cneg[:, 2 * k + t:2 * k + t + 1])
                    last.then_inc(sems["rth"], 1)
                    act.wait_ge(sems["rm"], k + 1)
                    nc.scalar.activation(pair(qk, 7), pair(qk, 6), ACT.Sqrt).then_inc(sems["rsb"], 1)

            def hy(s):
                L, ub, c = hys.index(s), B[s], s[-1]
                norm(s)
                if L == 0:
                    act.wait_ge(sems["geo_trig"], 1)
                    nc.scalar.activation(geo[:, 3], geo[:, 2], ACT.Sin)
                    nc.scalar.activation(half_sin, geo[:, 2], ACT.Sin, scale=0.5).then_inc(sems["geo_trig"], 1)
                act.wait_ge(sems["lam_exp"], 2 * L + 1)
                nc.scalar.activation(lamt[:, 2:4], lamt[:, 0:2], ACT.Exp).then_inc(sems["lam_exp"], 1)
                after(ub)
                evacuate(s, 0, ot[:, 0], pair(sq, 0))
                after(ub + 1)
                evacuate(s, 1, ot[:, 1], pair(sq, 1))
                for e in (2, 3, 4, 5):
                    after(ub + e)
                    if e == 2:
                        act.wait_ge(sems["cst_done"], 2 * L + 2)
                        for j, (dim, w) in enumerate(((256, 0), (128, 1))):
                            nc.scalar.activation(crs[:, j], bank[6][:, j * S:(j + 1) * S], ACT.Sqrt, bias=eps,
                                                 scale=1.0 / dim).then_inc(sems["crms"], 1)
                    evacuate(s, e, pair(qk, e - 2), set_slot(s, e - 2))
                act.wait_ge(sems["cf_done"], L + 1)
                nc.scalar.activation(y_hi[:, 0].rearrange("p a n -> p (a n)"), ot[:, 0], ACT.Copy)
                nc.scalar.activation(y_hi[:, 1, 0], ot[:, 1, 0:S], ACT.Copy).then_inc(sems["chi"], 1)
                for e in (6, 7):
                    after(ub + e)
                    token_values(s, e, 512 * (e - 6)).then_inc(sems["in_ev"], 1)
                    if e == 6:
                        set_root(s, 0, 64)
                for e in (8, 9):
                    after(ub + e)
                    evacuate(s, e, pair(qk, e - 4), set_slot(s, e - 4))
                after(ub + 10)
                act.wait_ge(sems["scaled"], scale_no(s, 10))
                token_values(s, 10, 2048, S, 128)
                b = bank[(total(s, "groups") + 10) % 2]
                nc.scalar.activation(qk[:, 12], b[:, 0:S], ACT.Copy)
                nc.scalar.activation(set_slot(s, 6)[:, 0:S], b[:, 0:S], ACT.Square).then_inc(sems["in_ev"], 1)
                sqs = lambda k: set_slot(s, k)
                evacuate(s, 11, qk[:, 13:15].rearrange("p a n -> p (a n)"), sqs(7))
                set_root(s, 1, 64)
                evacuate(s, 12, qk[:, 15:17].rearrange("p a n -> p (a n)"), sqs(8))
                after(ub + 11)
                evacuate(s, 13, qk[:, 17:19].rearrange("p a n -> p (a n)"), sqs(9))
                evacuate(s, 14, qk[:, 19:21].rearrange("p a n -> p (a n)"), sqs(10))
                evacuate(s, 15, qk[:, 21:23].rearrange("p a n -> p (a n)"), sqs(11))
                krs = sqs(12)
                nc.scalar.activation(krs[:, 0:S], cq[:, 3], ACT.Square).then_inc(sems["krsq"], 1)
                evacuate(s, 16, val[:, 1024:1536])
                after(ub + 12)
                evacuate(s, 17, val[:, 1536:2048])
                set_root(s, 2, 96)
                attention(s, {2 * j + 1: (ub + 13 + j, 18 + j, pair(wide, j)) for j in range(12)})
                act.wait_ge(sems["in_ev"], total(s, "groups") + 30)
                for b in range(3):
                    g = wide[:, 8 * b:8 * b + 8].rearrange("p a n -> p (a n)")
                    nc.scalar.activation(g, g, ACT.Sigmoid).then_inc(sems["sig_done"], 1)
                    if b:
                        branch_input(s, b + 1)
                branch_input(s, 4)
                branch_input(s, 5)
                after(ub + 29)
                for j in range(4):
                    act.wait_ge(sems["mg_up"], 4 * L + j + 1)
                    to_h(s, sq, j)
                for n in range(30, 34):
                    after(ub + n)

            def ple(s):
                L, ub = ples.index(s), B[s]

                def embedding():
                    for b in range(4):
                        acc_ready(act, s, 0, b)
                        nc.scalar.activation(pair(wide, b), bank[b][:], ACT.Copy)
                        nc.scalar.activation(pair(wide, 4 + b), bank[b][:], ACT.Square).then_inc(sems["ple_ev"], 1)

                norm(s, embedding)
                after(ub)
                act.wait_ge(sems["est_done"], L + 1)
                nc.scalar.activation(crs[:, 1], bank[7][:, 0:S], ACT.Sqrt, bias=eps, scale=1.0 / D).then_inc(sems["erms"], 1)
                for n in range(1, 4):
                    after(ub + n)
                for b in range(4):
                    act.wait_ge(sems["scaled"], scaled_before(s) + b + 1)
                    nc.scalar.activation(pair(wide, 8 + b), bank[b][:], ACT.Sigmoid).then_inc(sems["ple_ev"], 1)

            def hf_(s):
                L = int(s[-1])
                act.dma_start(val[:, 0:512], PE_T[L]).then_inc(sems["pe_in"], 16)
                norm(s)
                act.wait_ge(sems["pe_in"], 16 * (ffs_hf.index(s) + 1))
                nc.scalar.activation(y_hi[:, 1].rearrange("p a n -> p (a n)"), val[:, 0:512], ACT.Copy).then_inc(sems["pehi"], 1)
                ffn(s)

            act.wait_ge(sems["setup"], 1)
            act.wait_ge(sems["vec_in"], 16)
            for s in used:
                k = kind(s)
                if k == "ffn":
                    norm(s)
                    ffn(s)
                else:
                    {"pa": pa, "rg": rg, "hy": hy, "hf": hf_, "ple": ple}[k](s)

        @block.vector
        def _(dve):
            state = {"split": 0}
            link = Chain(dve, "dve_chain")
            V = nc.vector

            def split(n0, i=None):
                dve.wait_ge(sems["hi_done"], plus(n0 + 1, i, 6))
                V.tensor_tensor(w_lo[:, n0 % NW], raw[:, n0 % NRAW], w_hi[:, n0 % NW].bitcast(F32), ALU.subtract)\
                    .then_inc(sems["lo_done"], 1)

            def after(n, i=None):
                if i is None:
                    while state["split"] <= min(n + 3, N_UNITS - 1):
                        split(state["split"])
                        state["split"] += 1
                else:
                    split(n + 3, i)

            def low(s, j):
                dve.wait_ge(sems["hhi_done"], 4 * NORM[s] + j + 1)
                for t in (2 * j, 2 * j + 1):
                    last = V.scalar_tensor_tensor(out=h_lo[:, t], in0=x[:, t], scalar=v_(GAIN[s], t),
                                                  in1=h_hi[:, t].bitcast(F32), op0=ALU.mult, op1=ALU.subtract)
                last.then_inc(sems["h_ready"], 1)

            def onward(s, b):
                i = used.index(s) + 1
                behind = {0: [], 1: [0], 2: [1], 3: [2, 3]}
                if kind(s) == "ple":
                    behind = {0: [], 1: [], 2: [0, 1], 3: [2, 3]}
                if i < len(used):
                    for j in behind[b]:
                        low(used[i], j)

            def norm(s):
                k = NORM[s]
                if k == 0:
                    for j in range(4):
                        low(s, j)
                    after(-3)
                after(B[s] - 1)
                dve.wait_ge(sems["rms_done"], k + 1)
                w = S + 2 if s in atts else S
                V.reciprocal(rinv_t[:, 0:w], rinv_t[:, 0:w]).then_inc(sems["rinv_done"], 1)
                dve.wait_ge(sems["rinv_done"], k + 1)

            def scale(bk, w=2 * S):
                z = bk[:, 0:w].rearrange("p (a n) -> p a n", a=w // S)
                return V.tensor_tensor(z, z, rinv.unsqueeze(1).broadcast_to([P, w // S, S]), ALU.mult)\
                    .then_inc(sems["scaled"], 1)

            def scale_group(s, e):
                group_ready(dve, s, e)
                scale(bank[(total(s, "groups") + e) % 2], S if kind(s) == "hy" and e == 10 else 2 * S)

            def update(s, j):
                for b in range(4):
                    acc_ready(dve, s, j, b)
                    V.tensor_tensor(pair(x, b), pair(x, b), bank[b][:], ALU.add).then_inc(sems["x_up"], 1)
                    onward(s, b)

            def ffn(s):
                f, ub, causal = ffs.index(s), B[s], kind(s) == "ffn"
                cols = f"cf{s[-1]}" if causal else f"cg{s[-1]}"
                nt = 4 if causal else 2
                T = qk[:, 0:4, :]

                def conv(t, tap, sh, s0, i):
                    o = vec_at[cols][0] + 4 * (nt * s0 + t) + tap
                    w = vec[:, o:o + 1] if i is None else vec[:, bass.ds(i * (8 * nt) + o, 1)]
                    z = bank[4 + t // 2]
                    a = (t % 2) * S
                    dst = T[:, t, max(sh, 0):S + min(sh, 0)]
                    src = z[:, a + max(-sh, 0):a + S - max(sh, 0)]
                    return V.scalar_tensor_tensor(out=dst, in0=src, scalar=w, in1=dst, op0=ALU.mult, op1=ALU.add)

                taps = ((1, 1), (0, 2)) if causal else ((0, 1), (2, -1))

                def step(s0, i=None):
                    u = ub + (3 * s0 - 1 if s0 else 0)
                    done = lambda c: plus(FF_STEPS * f + s0 + c, i, 2)
                    cdone = lambda c: plus(FF_STEPS * causals.index(s) + s0 + c, i, 2)
                    dve.wait_ge(sems["w_used"], plus(u + 1, i, 6))
                    scale(bank[4])
                    late = parts_late(s, s0)
                    if not late and s0:
                        after(u, i)
                    dve.wait_ge(sems["tu"], done(1))
                    conv(0, *taps[0], s0, i)
                    link(conv(1, *taps[0], s0, i))
                    conv(0, *taps[1], s0, i)
                    conv(1, *taps[1], s0, i).then_inc(sems["cvu" if causal else "cvg"], 1)
                    if late or not s0:
                        after(u, i)
                    dve.wait_ge(sems["w_used"], plus(u + 2, i, 6))
                    scale(bank[5])
                    if not late:
                        after(u + 1, i)
                    if causal:
                        dve.wait_ge(sems["tg"], cdone(1))
                        conv(2, *taps[0], s0, i)
                        link(conv(3, *taps[0], s0, i))
                        conv(2, *taps[1], s0, i)
                        conv(3, *taps[1], s0, i).then_inc(sems["cvg"], 1)
                    dve.wait_ge(sems["gelu"], done(1))
                    if f or s0:
                        dve.wait_ge(sems["ffy"], done(0))
                    if causal:
                        up = pair(qk, 0)
                    else:
                        dve.wait_ge(sems["scaled"], plus(scaled_before(s) + 2 * s0 + 2, i, 4))
                        up = bank[5][:]
                    V.tensor_tensor(pair(qk, 3), pair(qk, 2), up, ALU.mult).then_inc(sems["ymul"], 1)
                    if late:
                        after(u + 1, i)
                    if s0:
                        after(u + 2, i)

                for s0 in range(3):
                    step(s0)
                with dve.Fori(0, LOOPED // 2) as i:
                    link.enter(i, 4 if causal else 2)
                    step(3, i)
                    step(4, i)
                link.leave(LOOPED // 2)
                state["split"] = ub + 3 * (3 + LOOPED) + 2
                for s0 in range(3 + LOOPED, FF_STEPS):
                    step(s0)
                update(s, 0)

            def set_scale(s, j, col):
                n = nsets(s) + j
                dve.wait_ge(sems["hroot"], n + 1)
                link(V.reciprocal(hr, hr))
                V.tensor_scalar(hr, hr, c_("scale_pair")[0:16, col:col + 1], None, ALU.mult)\
                    .then_inc(sems["hr_ready"], 1)

            def head_norm(s, k, tiles, gains):
                q = total(s, "pairs") + k
                dve.wait_ge(sems["bc_done"], q + 1)
                for j, (t, g) in enumerate(zip(tiles, gains)):
                    last = V.scalar_tensor_tensor(out=qk[:, t], in0=qk[:, t], scalar=g,
                                                  in1=bank[4 + q % 2][:, j * S:(j + 1) * S], op0=ALU.mult, op1=ALU.mult)
                last.then_inc(sems["qk_done"], 1)

            def logits(s, i):
                m, n = att_maps(s)[i], total(s, "maps") + i
                dve.wait_ge(sems["s_done"], n + 1)
                src = bank[4 + i % 2]
                if m["dist"]:
                    d = {"causal": pa_con[:, 0:2 * S], "win": c_("win_mask"),
                         "plain": geo[:, 0:2].rearrange("p a n -> p (a n)")}[m["dist"]]
                    link(V.scalar_tensor_tensor(out=lg[:, i % 2], in0=d, scalar=m["slope"], in1=src[:],
                                                op0=ALU.mult, op1=ALU.subtract))
                    red = V.tensor_reduce(nm[:, i], lg[:, i % 2].rearrange("p (a n) -> p a n", a=2), AX.X, ALU.min)
                    if m["sink"] is not None:
                        link(red)
                        red = V.tensor_scalar(nm[:, i], nm[:, i], nsink[:, m["sink"]:m["sink"] + 1], None, ALU.min)
                else:
                    red = V.tensor_reduce(nm[:, i], src[:].rearrange("p (a n) -> p a n", a=2), AX.X, ALU.max, negate=True)
                red.then_inc(sems["lp_done"], 1)

            def outputs(s, g):
                K, ms = kind(s), att_maps(s)
                mine = [i for i, m in enumerate(ms) if m["g"] == g]
                a, n, gg = mine[0], len(mine), total(s, "ogroups") + g
                dve.wait_ge(sems["pv_done"], gg + 1)
                if ms[a]["sink"] is not None:
                    h = ms[a]["sink"]
                    link(V.tensor_tensor(sums[:, a:a + n], sums[:, a:a + n], esink[:, h:h + n], ALU.add))
                link(V.reciprocal(rec[:, 0:n], sums[:, a:a + n]))
                O = bank[2 + gg % 2]
                pairs = total(s, "opairs")
                if K == "pa" or g >= 4:
                    p = g if K == "pa" else g - 2
                    if p >= 2:
                        dve.wait_ge(sems["pt_done"], use_no(s, ("pair", p - 2)) + 1)
                    src = O[:].rearrange("p (q h d) -> p q h d", q=2, h=4)
                    dst = ot[:, p % 2].rearrange("p (q h d) -> p q h d", q=2, h=4)
                    for q in range(2):
                        last = V.tensor_tensor(dst[:, q], src[:, q], rec[:, 0:4, q].unsqueeze(2).broadcast_to([P, 4, 64]),
                                               ALU.mult)
                    last.then_inc(sems["o_ev"], 1)
                    return
                h, L = g, hys.index(s)
                link(V.tensor_scalar(rec[:, 1], rec[:, 1], lamt[:, 4:5], None, ALU.mult))
                for q in range(2):
                    last = V.tensor_scalar(dtmp[:, q], O[:, q * S + 128:q * S + 256], rec[:, 1, q:q + 1], None, ALU.mult)
                link(last)
                od = ot[:, h // 2].rearrange("p (q h d) -> p q h d", q=2, h=2)[:, :, h % 2]
                for q in range(2):
                    last = V.scalar_tensor_tensor(out=od[:, q], in0=O[:, q * S:q * S + 128], scalar=rec[:, 0, q:q + 1],
                                                  in1=dtmp[:, q], op0=ALU.mult, op1=ALU.subtract)
                last.then_inc(sems["od_free"], 1)
                dve.wait_ge(sems["od_free"], 4 * L + h + 1)
                for q in range(2):
                    link(V.tensor_tensor(dtmp[:, q], od[:, q], od[:, q], ALU.mult))
                last = V.tensor_reduce(odss[:, h], dtmp, AX.X, ALU.add)
                if h == 3:
                    last.then_inc(sems["od_ss"], 1)

            def attention(s, fillers):
                n = PLAN[kind(s)]["maps"]
                logits(s, 0)
                for i in range(n + 1):
                    if i + 1 < n:
                        logits(s, i + 1)
                    if ended(s, i - 1) is not None:
                        outputs(s, ended(s, i - 1))
                    if kind(s) == "hy" and i == 9:
                        L = hys.index(s)
                        dve.wait_ge(sems["od_root"], L + 1)
                        link(V.reciprocal(odr[:], odr[:]))
                        link(V.tensor_scalar(odr[:], odr[:], 1.0 - LAM0[int(s[-1])], None, ALU.mult))
                        for p in range(2):
                            for q in range(2):
                                o = ot[:, p].rearrange("p (q h d) -> p q h d", q=2, h=2)[:, q]
                                last = V.tensor_tensor(o, o, odr[:, 2 * p:2 * p + 2, q].unsqueeze(2)
                                                       .broadcast_to([P, 2, 128]), ALU.mult)
                            last.then_inc(sems["o_ev"], 1)
                    if i in fillers:
                        scale_group(s, fillers[i][1])
                        after(fillers[i][0])

            def pa(s):
                ub = B[s]
                norm(s)
                for e in range(5):
                    if e < 4:
                        scale_group(s, e)
                    after(ub + e)
                set_scale(s, 0, 0)
                after(ub + 5)
                for k in range(4):
                    head_norm(s, k, (2 * k, 2 * k + 1), (v_("pa_gain", 2 * k), v_("pa_gain", 2 * k + 1)))
                dve.wait_ge(sems["pa_in"], 16)
                attention(s, {1: (ub + 6, 6), 3: (ub + 7, 7)})
                for n in range(8, 11):
                    after(ub + n)
                update(s, 0)

            def rg(s):
                ub = B[s]
                norm(s)
                for k in range(RG_STEPS):
                    u = ub + (3 * k - 1 if k else 0)
                    vb = lambda t, c: v_("rgv", 16 * k + 8 * t + c)
                    dve.wait_ge(sems["w_used"], u + 1)
                    scale(bank[4])
                    after(u)
                    dve.wait_ge(sems["w_used"], u + 2)
                    scale(bank[5])
                    if k:
                        after(u + 1)
                    dve.wait_ge(sems["rtx"], k + 1)
                    for sh in (1, 2, 3):
                        for t in range(2):
                            dst = qk[:, t, sh:S]
                            last = V.scalar_tensor_tensor(out=dst, in0=bank[5][:, t * S:(t + 1) * S - sh], scalar=vb(t, 3 - sh),
                                                          in1=dst, op0=ALU.mult, op1=ALU.add)
                        if sh < 3:
                            link(last)
                    last.then_inc(sems["xcv"], 1)
                    if k:
                        after(u + 2)
                    else:
                        after(u + 1)
                        dve.wait_ge(sems["rgc_act"], 2)
                        e, ln, u, msk, t = rgt[:, 1], rgt[:, 2], rgt[:, 3], rgt[:, 4], rgt[:, 5]
                        link(V.tensor_scalar(u, e, 1.0, -1.0, ALU.add, ALU.add))
                        link(V.tensor_scalar(msk, u, 0.0, None, ALU.is_equal))
                        link(V.tensor_tensor(u, u, msk, ALU.add))
                        link(V.tensor_tensor(ln, ln, msk, ALU.add))
                        link(V.reciprocal(u, u))
                        link(V.tensor_tensor(ln, ln, u, ALU.mult))
                        link(V.tensor_tensor(ln, ln, e, ALU.mult))
                        link(V.tensor_scalar(t, lamr, -1.0, 0.0, ALU.mult, ALU.max))
                        link(V.tensor_tensor(t, t, ln, ALU.add))
                        V.tensor_scalar(cpos[:], t, 8.0, None, ALU.mult)
                        V.tensor_scalar(cneg[:], t, -8.0, None, ALU.mult).then_inc(sems["rgc_ready"], 1)
                    dve.wait_ge(sems["rsig"], k + 1)
                    link(V.tensor_tensor(pair(qk, 8), pair(qk, 3), pair(qk, 0), ALU.mult))
                    dve.wait_ge(sems["rth"], k + 1)
                    link(V.tensor_tensor(pair(qk, 6), pair(qk, 5), pair(qk, 5), ALU.mult))
                    V.scalar_tensor_tensor(out=pair(qk, 6), in0=pair(qk, 6), scalar=1.0, in1=pair(qk, 4),
                                           op0=ALU.add, op1=ALU.mult).then_inc(sems["rm"], 1)
                    dve.wait_ge(sems["rsb"], k + 1)
                    link(V.tensor_tensor(pair(qk, 8), pair(qk, 8), pair(qk, 7), ALU.mult))
                    for t in range(2):
                        last = V.tensor_tensor_scan(qk[:, 18 + t], qk[:, 10 + t], qk[:, 16 + t], 0.0, ALU.mult, ALU.add)
                    link(last)
                    if k:
                        dve.wait_ge(sems["ry_ready"], k)
                    V.tensor_tensor(pair(qk, 10), pair(qk, 9), pair(qk, 1), ALU.mult).then_inc(sems["rgy"], 1)
                    dve.wait_ge(sems["rgy"], k + 1)
                    if k:
                        dve.wait_ge(sems["w_used"], u + 3)
                    V.tensor_copy(pair(y_hi[:, 0], 0), pair(qk, 10)).then_inc(sems["ryhi"], 1)
                update(s, 0)

            def geometry():
                dve.wait_ge(sems["pos_in"], 48)
                dve.wait_ge(sems["con_in"], 16)
                V.tensor_copy(posf, posr[:])
                link(V.tensor_copy(poscf[:], posc[:]))
                for q in range(2):
                    V.tensor_scalar(geo[:, q], posf, poscf[:, q:q + 1], None, ALU.subtract)
                    last = V.tensor_scalar(geo[:, 2 + q], posf, -1.0, poscf[:, q:q + 1], ALU.mult, ALU.add)
                link(last)
                link(V.tensor_tensor(pair(geo, 0), pair(geo, 0), pair(geo, 1), ALU.max))
                V.tensor_tensor(c_("win_mask"), c_("win_mask"), pair(geo, 0), ALU.add)
                A, K = geo[:, 2], geo[:, 3]
                link(V.tensor_scalar(A, posf, c_("freq"), None, ALU.mult))
                link(V.tensor_scalar(K, A, 1.0 / TWO_PI, ROUND, ALU.mult, ALU.add))
                link(V.tensor_scalar(K, K, ROUND, None, ALU.subtract))
                for part in TWO_PI_PARTS:
                    link(V.scalar_tensor_tensor(out=A, in0=K, scalar=-part, in1=A, op0=ALU.mult, op1=ALU.add))
                V.tensor_scalar(A, A, PI_LOW, -PI_LOW, ALU.min, ALU.max).then_inc(sems["geo_trig"], 1)

            def cosines():
                dve.wait_ge(sems["geo_trig"], 2)
                link(V.tensor_tensor(half_sin, half_sin, half_sin, ALU.mult))
                V.tensor_scalar(geo[:, 2], half_sin, -2.0, 1.0, ALU.mult, ALU.add).then_inc(sems["geo_ready"], 1)
                dve.wait_ge(sems["geo_ready"], 1)

            def rotate(dst, n, src_bank, rope):
                dve.wait_ge(sems["rope_mm"], rope + 1)
                tmp = lg[:, 0, 0:n * S].rearrange("p (a n) -> p a n", a=n)
                src = src_bank[:, 0:n * S].rearrange("p (a n) -> p a n", a=n)
                C = geo[:, 2].unsqueeze(1).broadcast_to([P, n, S])
                Z = geo[:, 3].unsqueeze(1).broadcast_to([P, n, S])
                V.tensor_tensor(tmp, src, Z, ALU.mult)
                link(V.tensor_tensor(dst, dst, C, ALU.mult))
                return V.tensor_tensor(dst, dst, tmp, ALU.add)

            def hy(s):
                L, ub, c = hys.index(s), B[s], s[-1]
                if L == 0:
                    geometry()
                norm(s)
                scale_group(s, 0)
                for j in range(2):
                    o = (int(c) * 4 + 2 * j) * 64
                    link(V.tensor_tensor(lamp[:, j], lamv[:, o:o + 64], lamv[:, o + 64:o + 128], ALU.mult))
                V.tensor_reduce(lamt[:, 0:2], lamp, AX.X, ALU.add).then_inc(sems["lam_exp"], 1)
                V.tensor_scalar(nsink[:], v_(f"sink{c}", 0, 8), -1.0, None, ALU.mult)
                if L == 0:
                    cosines()
                dve.wait_ge(sems["lam_exp"], 2 * L + 2)
                link(V.tensor_tensor(lamt[:, 4:5], lamt[:, 2:3], lamt[:, 3:4], ALU.subtract))
                link(V.tensor_scalar(lamt[:, 4:5], lamt[:, 4:5], LAM0[int(c)], None, ALU.add))
                after(ub)
                scale_group(s, 1)
                after(ub + 1)
                for e in range(2, 6):
                    scale_group(s, e)
                    after(ub + e)
                for j, tiles in ((0, (0, 1)), (1, (2,))):
                    dve.wait_ge(sems["crms"], 2 * L + j + 1)
                    link(V.reciprocal(crs[:, j], crs[:, j]))
                    for t in tiles:
                        last = V.scalar_tensor_tensor(out=cq[:, t], in0=cq[:, t],
                                                      scalar=v_(f"g_cq{c}", t) if j == 0 else v_(f"g_ckv{c}"),
                                                      in1=crs[:, j], op0=ALU.mult, op1=ALU.mult)
                last.then_inc(sems["cf_done"], 1)
                V.tensor_scalar(crs[:, 2], cq[:, 3], v_(f"g_krope{c}"), None, ALU.mult).then_inc(sems["kro_done"], 1)
                after(ub + 6)
                set_scale(s, 0, 0)
                after(ub + 7)
                scale_group(s, 8)
                after(ub + 8)
                for k in range(4):
                    head_norm(s, k, (2 * k, 2 * k + 1), (v_(f"g_diff{c}", 2 * k), v_(f"g_diff{c}", 2 * k + 1)))
                scale_group(s, 9)
                after(ub + 9)
                scale_group(s, 10)
                after(ub + 10)
                set_scale(s, 1, 1)
                after(ub + 11)
                gw = lambda t: v_(f"g_win{c}", t)
                head_norm(s, 4, (8, 9), (gw(0), gw(1)))
                head_norm(s, 5, (10, 11), (gw(2), gw(3)))
                head_norm(s, 6, (12,), (gw(4),))
                dve.wait_ge(sems["kro_done"], 2 * L + 1)
                rotate(crs[:, 2:3], 1, bank[7], 2 * L).then_inc(sems["kro_done"], 1)
                after(ub + 12)
                set_scale(s, 2, 2)
                gm = lambda t: v_(f"g_mla{c}", t)
                head_norm(s, 7, (13, 14), (gm(0), gm(1)))
                head_norm(s, 8, (15, 16), (gm(2), gm(3)))
                head_norm(s, 9, (17, 18), (gm(4), gm(5)))
                head_norm(s, 10, (19, 20), (gm(6), gm(7)))
                head_norm(s, 11, (21, 22), (gm(8), gm(9)))
                q = total(s, "pairs") + 12
                dve.wait_ge(sems["bc_done"], q + 1)
                dve.wait_ge(sems["kro_done"], 2 * L + 2)
                V.tensor_tensor(qk[:, 23:25], crs[:, 2:3].broadcast_to([P, 2, S]),
                                bank[4 + q % 2][:].rearrange("p (a n) -> p a n", a=2), ALU.mult).then_inc(sems["qk_done"], 1)
                rotate(qk[:, 17:19], 2, bank[7], 2 * L + 1).then_inc(sems["rope_done"], 1)
                attention(s, {2 * j + 1: (ub + 13 + j, 18 + j) for j in range(12)})
                for b in range(3):
                    dve.wait_ge(sems["sig_done"], 3 * L + b + 1)
                    after(ub + 25 + 2 * b)
                    for j in range(4):
                        acc_ready(dve, s, b, j)
                        g = pair(wide, 4 * b + j)
                        V.tensor_tensor(g if b else pair(sq, j), g, bank[j][:], ALU.mult).then_inc(sems["br_up"], 1)
                        if b:
                            dve.wait_ge(sems["br_up"], 12 * L + 4 * b + j + 1)
                            last = V.tensor_tensor(pair(sq, j), pair(sq, j), g, ALU.add)
                            if b == 2:
                                last.then_inc(sems["mg_up"], 1)
                            elif j == 3:
                                link(last)
                    after(ub + 26 + 2 * b)
                for u in range(31, 34):
                    after(ub + u)
                update(s, 3)

            def ple(s):
                L, ub = ples.index(s), B[s]
                norm(s)
                after(ub)
                dve.wait_ge(sems["erms"], L + 1)
                link(V.reciprocal(crs[:, 1], crs[:, 1]))
                for t in range(8):
                    last = V.scalar_tensor_tensor(out=wide[:, t], in0=wide[:, t], scalar=v_(f"g_ple{s[-1]}", t), in1=crs[:, 1],
                                                  op0=ALU.mult, op1=ALU.mult)
                link(last)
                for u in range(1, 4):
                    after(ub + u)
                acc_ready(dve, s, 1, 0)
                scale(bank[0])
                for b in range(4):
                    if b < 3:
                        acc_ready(dve, s, 1, b + 1)
                        scale(bank[b + 1])
                    dve.wait_ge(sems["ple_ev"], 8 * L + 5 + b)
                    link(V.tensor_tensor(pair(wide, 8 + b), pair(wide, 8 + b), pair(wide, b), ALU.mult))
                    V.tensor_tensor(pair(x, b), pair(x, b), pair(wide, 8 + b), ALU.add).then_inc(sems["x_up"], 1)
                    onward(s, b)

            V.memset(eps, EPS).then_inc(sems["setup"], 1)
            dve.wait_ge(sems["vec_in"], 16)
            dve.wait_ge(sems["x_in"], 16)
            for s in used:
                k = kind(s)
                if k in ("ffn", "hf"):
                    norm(s)
                    ffn(s)
                else:
                    {"pa": pa, "rg": rg, "hy": hy, "ple": ple}[k](s)

        @block.gpsimd
        def _(pool):
            link = Chain(pool, "pool_chain")
            G = nc.gpsimd

            def low(dst, src, hi):
                return G.tensor_tensor(dst, src, hi.bitcast(F32), ALU.subtract)

            def ffn(s):
                f = ffs.index(s)
                with pool.Fori(0, FF_STEPS) as i:
                    pool.wait_ge(sems["yhi"], i + (FF_STEPS * f + 1))
                    low(pair(y_lo[:, 0], 0), pair(qk, 3), pair(y_hi[:, 0], 0)).then_inc(sems["ffy"], 1)

            def to_h(s, src):
                a = atts.index(s)
                for j in range(4):
                    pool.wait_ge(sems["h2hi"], 4 * a + j + 1)
                    low(pair(h_lo, j), pair(src, j), pair(h_hi, j)).then_inc(sems["h2_ready"], 1)

            def pooling(s):
                pool.wait_ge(sems["in_ev"], total(s, "groups") + 8)
                pool.wait_ge(sems["pa_in"], 16)
                cur, nxt = pool_u, pool_a
                for lv in range(4):
                    sh = 2 ** lv
                    link(G.tensor_tensor(nxt[:, lv:4, 8:8 + S], cur[:, lv:4, 8:8 + S], cur[:, lv:4, 8 - sh:8 - sh + S], ALU.add))
                    cur, nxt = nxt, (pool_b if nxt is pool_a else pool_a)
                for g in range(4):
                    r = (pool_a if g % 2 == 0 else pool_b)[:, g, 8:8 + S]
                    link(G.tensor_tensor(r, r, pa_con[:, (2 + g) * S:(3 + g) * S], ALU.mult))
                    last = G.tensor_tensor(pool_u[:, g, 8:8 + S], r, pool_u[:, g, 8:8 + S], ALU.subtract)
                last.then_inc(sems["pool_p"], 1)

            if "pa" in used:
                for t in (pool_u, pool_a, pool_b):
                    last = G.memset(t[:, :, 0:8], 0.0)
                link(last)
            for s in used:
                k = kind(s)
                if k == "pa":
                    pooling(s)
                    to_h(s, hf)
                elif k in ("ffn", "hf"):
                    if k == "hf":
                        pool.wait_ge(sems["pehi"], ffs_hf.index(s) + 1)
                        low(y_lo[:, 1].rearrange("p a n -> p (a n)"), val[:, 0:512], y_hi[:, 1].rearrange("p a n -> p (a n)"))\
                            .then_inc(sems["pe_ready"], 1)
                    ffn(s)
                elif k == "rg":
                    for q in range(RG_STEPS):
                        pool.wait_ge(sems["ryhi"], q + 1)
                        low(pair(y_lo[:, 0], 0), pair(qk, 10), pair(y_hi[:, 0], 0)).then_inc(sems["ry_ready"], 1)
                elif k == "hy":
                    L = hys.index(s)
                    pool.wait_ge(sems["chi"], L + 1)
                    low(y_lo[:, 0].rearrange("p a n -> p (a n)"), ot[:, 0], y_hi[:, 0].rearrange("p a n -> p (a n)"))
                    low(y_lo[:, 1, 0], ot[:, 1, 0:S], y_hi[:, 1, 0]).then_inc(sems["c_ready"], 1)
                    for p in range(6):
                        pool.wait_ge(sems["bhi"], 6 * L + p + 1)
                        low(y_lo[:, p % 2].rearrange("p a n -> p (a n)"), ot_tiles(s, p), y_hi[:, p % 2].rearrange("p a n -> p (a n)"))\
                            .then_inc(sems["b_ready"], 1)
                    to_h(s, sq)

        @block.tensor
        def _(pe):
            T = nc.tensor
            ones = c_("ones")

            def three(out, w, a, start, stop, **kw):
                T.matmul(out, w[0], a[0], start=start, stop=False, **kw)
                T.matmul(out, w[0], a[1], start=False, stop=False, **kw)
                return T.matmul(out, w[1], a[0], start=False, stop=stop, **kw)

            def cols(n, a, w):
                return w_hi[:, n % NW, a:a + w], w_lo[:, n % NW, a:a + w]

            def unit(n, i=None):
                pe.wait_ge(sems["lo_done"], plus(n + 1, i, 6))

            def column_tile(n, t, out, last=None):
                for k in range(8):
                    m = three(out, cols(n, k * 256 + t * 128, 128), (h_hi[:, k], h_lo[:, k]), k == 0, k == 7)
                return m

            def token_tile(n, kt, c0, w, out):
                for k in range(8):
                    tok = slice(kt * 128, kt * 128 + 128)
                    m = three(out, (h_hi[:, k, tok], h_lo[:, k, tok]), cols(n, k * 256 + c0, w), k == 0, k == 7)
                return m

            def first_unit(s, out):
                n = B[s]
                unit(n)
                for k in range(8):
                    pe.wait_ge(sems["h_ready"], 4 * NORM[s] + k // 2 + 1)
                    for t in range(2):
                        m = three(out[:, t * S:(t + 1) * S], cols(n, k * 256 + t * 128, 128), (h_hi[:, k], h_lo[:, k]),
                                  k == 0 and t == 0, k == 7, skip_group_check=True)
                m.then_inc(sems["w_used"], 1)
                normed(s)

            def normed(s):
                k = NORM[s]
                if k == 0:
                    pe.wait_ge(sems["con_in"], 16)
                for t in range(8):
                    pe.wait_ge(sems["sq_ready"], 4 * k + t // 2 + 1)
                    m = T.matmul(bank[6][:, 0:S], ones, sq[:, t], start=t == 0, stop=t == 7)
                if s in atts:
                    for kt in range(2):
                        for t in range(8):
                            m = T.matmul(bank[6][:, S + kt:S + kt + 1], sq[:, t, kt * P:(kt + 1) * P], ones[:, 0:1],
                                         start=t == 0, stop=t == 7)
                m.then_inc(sems["st_done"], 1)

            def onto(s, j, n, act_parts, begin, end, i=None, free=True):
                unit(n, i)
                for m in range(8):
                    if begin and m % 2 == 0 and free:
                        acc_free(pe, s, j, m // 2)
                    for k in range(2):
                        last = three(bank[m // 2][:, (m % 2) * S:(m % 2 + 1) * S], cols(n, k * 1024 + m * 128, 128),
                                     act_parts[k], begin and m % 2 == 0 and k == 0, end and k == 1, skip_group_check=True)
                    if end and m in (1, 3, 5):
                        last.then_inc(sems["acc_done"], 1)
                last.then_inc(sems["w_used"], 1)

            def y_parts(slot):
                return [(y_hi[:, slot, k], y_lo[:, slot, k]) for k in range(2)]

            def h_parts(j):
                return [(h_hi[:, 2 * j + k], h_lo[:, 2 * j + k]) for k in range(2)]

            def ffn(s):
                f, ub, causal = ffs.index(s), B[s], kind(s) == "ffn"

                def step(s0, i=None):
                    u = ub + (3 * s0 - 1 if s0 else 0)
                    done = lambda c: plus(FF_STEPS * f + s0 + c, i, 2)
                    if s0:
                        unit(u, i)
                        if causal:
                            pe.wait_ge(sems["cvu"], plus(FF_STEPS * causals.index(s) + s0, i, 2))
                        else:
                            pe.wait_ge(sems["cvg"], done(0))
                        column_tile(u, 0, bank[4][:, 0:S])
                        column_tile(u, 1, bank[4][:, S:2 * S]).then_inc(sems["w_used"], 1)
                    else:
                        first_unit(s, bank[4])
                    unit(u + 1, i)
                    if s0:
                        pe.wait_ge(sems["cvg" if causal else "ymul"], done(0))
                    column_tile(u + 1, 0, bank[5][:, 0:S])
                    column_tile(u + 1, 1, bank[5][:, S:2 * S]).then_inc(sems["w_used"], 1)
                    if s0:
                        pe.wait_ge(sems["ffy"], done(0))
                        onto(s, 0, u + 2, y_parts(0), s0 == 1, False, i)

                for s0 in range(3):
                    step(s0)
                with pe.Fori(0, LOOPED // 2) as i:
                    step(3, i)
                    step(4, i)
                for s0 in range(3 + LOOPED, FF_STEPS):
                    step(s0)
                pe.wait_ge(sems["ffy"], FF_STEPS * (f + 1))
                onto(s, 0, ub + 32, y_parts(0), False, True)

            def group_bank(s, e):
                g = total(s, "groups") + e
                if g >= 2:
                    pe.wait_ge(sems["in_ev"], g - 1)
                return bank[g % 2]

            def feature_unit(s, n, e):
                unit(n)
                b = group_bank(s, e)
                column_tile(n, 0, b[:, 0:S])
                column_tile(n, 1, b[:, S:2 * S]).then_inc(sems["w_used"], 1)

            def token_unit(s, n, e):
                unit(n)
                b = group_bank(s, e)
                token_tile(n, 0, 0, 256, b[:, 0:S])
                token_tile(n, 1, 0, 256, b[:, S:2 * S]).then_inc(sems["w_used"], 1)

            def set_stat(s, j, k, tiles, group, first_, last_, before=None):
                if group is not None:
                    pe.wait_ge(sems["in_ev"], total(s, "groups") + group + 1)
                if first_ and before:
                    pe.wait_ge(sems[before[0]], before[1])
                for a, (sel, t) in enumerate(tiles):
                    end = last_ and a == len(tiles) - 1
                    m = T.matmul(bank[6][0:16, 0:S], sel, sq[:, (2 * k + t) % 8], start=first_ and a == 0, stop=end)
                m.then_inc(sems["hst_mm"], 1)

            def heads(t):
                return c_("pick")[:, 14 - 2 * t:30 - 2 * t]

            def ropes(t):
                return c_("rpick")[:, 4 - 4 * t:20 - 4 * t]

            def broadcast(s, j, k, sels):
                q = total(s, "pairs") + k
                pe.wait_ge(sems["hr_ready"], nsets(s) + j + 1)
                if q >= 2:
                    pe.wait_ge(sems["qk_done"], q - 1)
                for a, sel in enumerate(sels):
                    m = T.matmul(bank[4 + q % 2][:, a * S:(a + 1) * S], sel, hr, start=True, stop=True)
                m.then_inc(sems["bc_done"], 1)

            def spread(t):
                return c_("spread")[0:16, t * P:(t + 1) * P]

            def rspread(t):
                return c_("rspread")[0:16, t * P:(t + 1) * P]

            def scores(s, i):
                m = att_maps(s)[i]
                b = bank[4 + i % 2]
                for qt in range(2):
                    n = len(m["q"])
                    for a, ((tq, p, w), (tk, _, _)) in enumerate(zip(m["q"], m["k"])):
                        last = T.matmul(b[:, qt * S:(qt + 1) * S], qk[p:p + w, tq, qt * P:(qt + 1) * P], qk[p:p + w, tk],
                                        start=a == 0, stop=a == n - 1)
                last.then_inc(sems["s_done"], 1)

            def transposed(s, u):
                n = use_no(s, u)
                if n >= 2:
                    pe.wait_ge(sems["pt_ev"], n - 1)
                b = bank[6 + n % 2]
                if u[0] == "map":
                    pe.wait_ge(sems["exp_done"], total(s, "maps") + u[1] + 1)
                    src = lg[:, u[1] % 2]
                else:
                    pe.wait_ge(sems["o_ev"], total(s, "opairs") + u[1] + 1)
                    src = ot[:, u[1] % 2]
                for qt in range(2):
                    for kt in range(2):
                        m = T.transpose(b[:, kt * S + qt * P:kt * S + qt * P + P], src[:, qt * S + kt * P:qt * S + kt * P + P],
                                        c_("ident"))
                m.then_inc(sems["pt_done"], 1)

            def outputs(s, i):
                m = att_maps(s)[i]
                g = total(s, "ogroups") + m["g"]
                if m["slot"] == 0 and m["g"] >= 2:
                    if kind(s) == "hy" and m["g"] - 2 < 4:
                        pe.wait_ge(sems["od_free"], 4 * hys.index(s) + m["g"] - 1)
                    else:
                        pe.wait_ge(sems["o_ev"], total(s, "opairs") + m["g"] - 2 - 2 + 1)
                pe.wait_ge(sems["pt_ev"], use_no(s, ("map", i)) + 1)
                b = bank[2 + g % 2]
                for qt in range(2):
                    o = b[:, qt * S + m["slot"] * m["w"]:qt * S + (m["slot"] + 1) * m["w"]]
                    for kt in range(2):
                        last = T.matmul(o, pt[:, i % 2, kt * S + qt * P:kt * S + qt * P + P], value(m["v"], kt),
                                        start=kt == 0, stop=kt == 1)
                if ended(s, i) is not None:
                    last.then_inc(sems["pv_done"], 1)

            def attention(s, fill):
                n = PLAN[kind(s)]["maps"]
                scores(s, 0)
                for i in range(n + 1):
                    if i + 1 < n:
                        scores(s, i + 1)
                    if i < n:
                        fill(i)
                    if i:
                        outputs(s, i - 1)
                    for u in uses(s, i):
                        transposed(s, u)

            def half_units(s, n0, e0, count):
                def fill(i):
                    if i >= 2 * count:
                        return
                    n, e = n0 + i // 2, e0 + i // 2
                    if i % 2 == 0:
                        unit(n)
                        group_bank(s, e)
                    m = column_tile(n, i % 2, bank[(total(s, "groups") + e) % 2][:, (i % 2) * S:(i % 2 + 1) * S])
                    if i % 2:
                        m.then_inc(sems["w_used"], 1)
                return fill

            def pa(s):
                ub = B[s]
                first_unit(s, bank[0])
                for e in range(1, 4):
                    feature_unit(s, ub + e, e)
                token_unit(s, ub + 4, 4)
                for k in range(4):
                    set_stat(s, 0, k, [(heads(2 * k), 0), (heads(2 * k + 1), 1)], k, k == 0, k == 3)
                token_unit(s, ub + 5, 5)
                for k in range(4):
                    broadcast(s, 0, k, (spread(2 * k), spread(2 * k + 1)))
                pe.wait_ge(sems["qk_done"], total(s, "pairs") + 4)
                pe.wait_ge(sems["in_ev"], total(s, "groups") + 6)
                attention(s, half_units(s, ub + 6, 6, 2))
                pe.wait_ge(sems["pool_p"], 1)
                pe.wait_ge(sems["pool_in"], 16)
                for g in range(4):
                    m = T.matmul(bank[g // 2][:, (g % 2) * S:(g % 2 + 1) * S],
                                 wide[:, 13:15].rearrange("p a n -> p (a n)")[:, g * P:(g + 1) * P], pool_u[:, g, 8:8 + S],
                                 start=True, stop=True)
                    if g % 2:
                        m.then_inc(sems["pm_done"], 1)
                pe.wait_ge(sems["psc"], 2)
                for j in range(4):
                    pe.wait_ge(sems["h2_ready"], 4 * atts.index(s) + j + 1)
                    onto(s, 0, ub + 8 + j, h_parts(j), j == 0, j == 3)

            def rg(s):
                ub = B[s]
                rw = wide[:, 0:10].rearrange("p a n -> p (a n)")
                for k in range(RG_STEPS):
                    u = ub + (3 * k - 1 if k else 0)
                    if k:
                        unit(u)
                        pe.wait_ge(sems["rgelu"], k)
                        column_tile(u, 0, bank[4][:, 0:S])
                        column_tile(u, 1, bank[4][:, S:2 * S]).then_inc(sems["w_used"], 1)
                    else:
                        first_unit(s, bank[4])
                        pe.wait_ge(sems["rg_in"], 16)
                    unit(u + 1)
                    if k:
                        pe.wait_ge(sems["xcv"], k)
                    column_tile(u + 1, 0, bank[5][:, 0:S])
                    column_tile(u + 1, 1, bank[5][:, S:2 * S]).then_inc(sems["w_used"], 1)
                    if k:
                        pe.wait_ge(sems["ry_ready"], k)
                        onto(s, 0, u + 2, y_parts(0), k == 1, False)
                    pe.wait_ge(sems["xcv"], k + 1)
                    if k:
                        pe.wait_ge(sems["rsig"], k)
                    for w in range(4):
                        m = T.matmul(bank[6 + w // 2][:, (w % 2) * S:(w % 2 + 1) * S],
                                     rw[:, (4 * k + w) * P:(4 * k + w + 1) * P], qk[:, w % 2], start=True, stop=True)
                    m.then_inc(sems["rmm"], 1)
                pe.wait_ge(sems["ry_ready"], RG_STEPS)
                onto(s, 0, ub + 14, y_parts(0), False, True)

            def hy(s):
                L, ub = hys.index(s), B[s]
                g0, hp, ns = total(s, "groups"), total(s, "pairs"), nsets(s)
                first_unit(s, bank[0])
                feature_unit(s, ub + 1, 1)
                for e in range(2, 6):
                    feature_unit(s, ub + e, e)
                    if e == 2:
                        pe.wait_ge(sems["in_ev"], g0 + 2)
                        for t in range(2):
                            m = T.matmul(bank[6][:, 0:S], ones, sq[:, t], start=t == 0, stop=t == 1)
                        m.then_inc(sems["cst_done"], 1)
                        T.matmul(bank[6][:, S:2 * S], ones, sq[:, 2], start=True, stop=True).then_inc(sems["cst_done"], 1)
                token_unit(s, ub + 6, 6)
                for k in range(4):
                    set_stat(s, 0, k, [(heads(2 * k), 0), (heads(2 * k + 1), 1)], 2 + k, k == 0, k == 3, ("crms", 2 * L + 2))
                pe.wait_ge(sems["kro_done"], 2 * L + 1)
                T.matmul(bank[7][:, 0:S], c_("perm"), crs[:, 2], start=True, stop=True).then_inc(sems["rope_mm"], 1)
                token_unit(s, ub + 7, 7)
                feature_unit(s, ub + 8, 8)
                for k in range(2):
                    broadcast(s, 0, k, (spread(2 * k), spread(2 * k + 1)))
                feature_unit(s, ub + 9, 9)
                for k in range(2, 4):
                    broadcast(s, 0, k, (spread(2 * k), spread(2 * k + 1)))
                unit(ub + 10)
                b = group_bank(s, 10)
                column_tile(ub + 10, 0, b[:, 0:S])
                token_tile(ub + 10, 0, 128, 128, b[:, S:S + 128])
                token_tile(ub + 10, 1, 128, 128, b[:, S + 128:2 * S]).then_inc(sems["w_used"], 1)
                pe.wait_ge(sems["c_ready"], L + 1)
                unit(ub + 11)
                for e in range(11, 14):
                    b = group_bank(s, e)
                    for t in range(2):
                        for k in range(2):
                            m = three(b[:, t * S:(t + 1) * S], cols(ub + 11, k * 1024 + (2 * (e - 11) + t) * P, P),
                                      (y_hi[:, 0, k], y_lo[:, 0, k]), k == 0, k == 1)
                    m.then_inc(sems["grp_done" if e < 13 else "w_used"], 1)
                    if e == 11:
                        for k in range(3):
                            set_stat(s, 1, 4 + k, [(heads(2 * k), 0), (heads(2 * k + 1), 1)][:2 if k < 2 else 1], 8 + k,
                                     k == 0, k == 2, ("hroot", ns + 1))
                mla = [[(heads(0), 0), (heads(1), 1)], [(heads(2), 0), (heads(3), 1)], [(ropes(0), 0), (ropes(1), 1)],
                       [(heads(4), 0), (heads(5), 1)], [(heads(6), 0), (heads(7), 1)]]
                for k in range(2):
                    set_stat(s, 2, 7 + k, mla[k], 11 + k, k == 0, False, ("hroot", ns + 2))
                unit(ub + 12)
                for e in (14, 15):
                    b = group_bank(s, e)
                    for t in range(2):
                        m = three(b[:, t * S:(t + 1) * S], cols(ub + 12, (2 * (e - 14) + t) * P, P),
                                  (y_hi[:, 1, 0], y_lo[:, 1, 0]), True, True)
                    m.then_inc(sems["grp_done"], 1)
                for kt in range(2):
                    b = group_bank(s, 16 + kt)
                    tok = slice(kt * P, kt * P + P)
                    m = three(b[:, 0:512], (y_hi[:, 1, 0, tok], y_lo[:, 1, 0, tok]), cols(ub + 12, 512, 512), True, True)
                    m.then_inc(sems["grp_done" if kt == 0 else "w_used"], 1)
                for k, sels in enumerate(((spread(0), spread(1)), (spread(2), spread(3)), (spread(4),))):
                    broadcast(s, 1, 4 + k, sels)
                for k in range(2, 5):
                    set_stat(s, 2, 7 + k, mla[k], 11 + k, False, False)
                pe.wait_ge(sems["krsq"], L + 1)
                set_stat(s, 2, 12, [(c_("kpick"), 0)], None, False, True)
                for k, sels in enumerate(((spread(0), spread(1)), (spread(2), spread(3)), (rspread(0), rspread(1)),
                                          (spread(4), spread(5)), (spread(6), spread(7)), (rspread(2), rspread(3)))):
                    broadcast(s, 2, 7 + k, sels)
                pe.wait_ge(sems["qk_done"], hp + 13)
                for t in range(2):
                    m = T.matmul(bank[7][:, t * S:(t + 1) * S], c_("perm"), qk[:, 17 + t], start=True, stop=True)
                m.then_inc(sems["rope_mm"], 1)
                pe.wait_ge(sems["in_ev"], g0 + 18)
                pe.wait_ge(sems["rope_done"], L + 1)
                attention(s, half_units(s, ub + 13, 18, 12))
                for b in range(3):
                    for j in range(2):
                        p = 2 * b + j
                        pe.wait_ge(sems["b_ready"], 6 * L + p + 1)
                        if p == 0:
                            pe.wait_ge(sems["in_ev"], g0 + 30)
                            pe.wait_ge(sems["o_ev"], total(s, "opairs") + 6)
                        onto(s, b, ub + 25 + p, y_parts(p % 2), j == 0, j == 1)
                for j in range(4):
                    pe.wait_ge(sems["h2_ready"], 4 * atts.index(s) + j + 1)
                    onto(s, 3, ub + 31 + j, h_parts(j), j == 0, j == 3)

            def ple(s):
                L, ub = ples.index(s), B[s]
                pe.wait_ge(sems["pe_ready"], L + 1)
                onto(s, 0, ub, y_parts(1), True, True)
                normed(s)
                pe.wait_ge(sems["ple_ev"], 8 * L + 4)
                for t in range(8):
                    m = T.matmul(bank[7][:, 0:S], ones, wide[:, 8 + t], start=t == 0, stop=t == 7)
                m.then_inc(sems["est_done"], 1)
                for j in range(4):
                    pe.wait_ge(sems["h_ready"], 4 * NORM[s] + j + 1)
                    onto(s, 1, ub + 1 + j, h_parts(j), j == 0, j == 3)

            for s in used:
                k = kind(s)
                if k in ("ffn", "hf"):
                    ffn(s)
                else:
                    {"pa": pa, "rg": rg, "hy": hy, "ple": ple}[k](s)


def const_table():
    import numpy as np
    at, width = columns(CONSTS)
    c = np.zeros((P, width), np.float32)

    def put(name, a):
        o, w = at[name]
        a = np.asarray(a, np.float32).reshape(a.shape[0], -1)
        c[:a.shape[0], o:o + a.shape[1]] = a

    p = np.arange(P)
    put("ident", np.eye(P))
    put("ones", np.ones((P, P)))
    perm = np.zeros((P, P))
    for q in range(P):
        j = q % 32
        perm[q + 16 if j < 16 else q - 16, q] = -1.0 if j < 16 else 1.0
    put("perm", perm)
    pick = np.zeros((P, 32))
    pick[:, 14], pick[:, 15] = p < 64, p >= 64
    put("pick", pick)
    rpick = np.zeros((P, 32))
    for j in range(4):
        rpick[:, 4 + j] = p // 32 == j
    put("rpick", rpick)
    kpick = np.zeros((P, 16))
    kpick[:32, 8:16] = 1
    put("kpick", kpick)
    put("spread", (np.arange(16)[:, None] == np.arange(8 * P)[None] // 64).astype(np.float32))
    put("rspread", (np.arange(16)[:, None] == np.arange(4 * P)[None] // 32).astype(np.float32))
    q = (p[:, None, None] + P * np.arange(2)[None, :, None])
    k = np.arange(S)[None, None, :]
    put("win_mask", np.where(np.abs(q - k) <= 128, 0.0, 1e30))
    half = 16
    freq = np.float32(10000.0) ** (-np.arange(half, dtype=np.float32) / np.float32(half))
    put("freq", freq[p % 16][:, None])
    sc = np.ones((16, 3))
    sc[:8, 0] = sc[:8, 1] = 64.0 ** -0.5
    sc[:8, 2] = 96.0 ** -0.5
    put("scale_pair", sc)
    t = np.arange(S)
    inv = np.stack([1.0 / np.minimum(t + 1, w) for w in (2, 4, 8, 16)]).reshape(1, -1)
    c0 = np.concatenate([np.where(q >= k, q - k, 1e30).reshape(P, -1), np.broadcast_to(inv, (P, 4 * S))], 1)
    return c, c0.astype(np.float32)


def kernel(**a):
    import numpy as np
    import concourse.bacc as bacc
    from concourse import mybir as mb
    from concourse.bass_utils import run_bass_kernel_spmd as run
    a = {k: np.ascontiguousarray(v) for k, v in a.items()}
    f32 = np.float32

    def iunit(w, c):
        return w[:, c].reshape(8, P, 256).transpose(1, 0, 2).reshape(P, UW)

    def ounit(w, j):
        return w[256 * j:256 * j + 256].reshape(2, P, 1024).transpose(1, 0, 2).reshape(P, UW)

    def r(o, n=256):
        return np.arange(o, o + n)

    units = []

    def steps(a_of, b_of, w_out, n):
        for k in range(n + 1):
            if k < n:
                units.append(a_of(k))
                units.append(b_of(k))
            if k:
                units.append(ounit(w_out, k - 1))

    w = a["pa_w_in"][0]
    for o in (512, 768, 1024, 1280, 1536, 1792, 0, 256):
        units.append(iunit(w, r(o)))
    for j in range(4):
        units.append(ounit(a["pa_w_out"][0], j))

    def ffn(L):
        wi = a["ffn_w_in"][L]
        steps(lambda k: iunit(wi, r(256 * k)), lambda k: iunit(wi, r(2816 + 256 * k)), a["ffn_w_out"][L], FF_STEPS)

    ffn(0)
    wr = a["rg_w_in"][0]
    steps(lambda k: iunit(wr, r(256 * k)), lambda k: iunit(wr, r(1280 + 256 * k)), a["rg_w_out"][0], RG_STEPS)
    ffn(1)
    for L in range(2):
        w = a["w_in_2"][L]
        kr = r(384, 32)
        heads = np.concatenate([r(1952 + 64 * h, 64) for h in (0, 4, 1, 5, 2, 6, 3, 7)])
        units.append(iunit(w, r(0)))
        units.append(iunit(w, np.concatenate([r(256, 128), kr, kr, kr, kr])))
        for o in (416, 672, 928, 1184, 1440, 1696):
            units.append(iunit(w, r(o)))
        units.append(iunit(w, heads[:256]))
        units.append(iunit(w, heads[256:]))
        units.append(iunit(w, r(2464)))
        uq = a["w_uq_2"][L].reshape(2, P, 8, 96)
        u = np.zeros((P, 2, 1024), f32)
        for k in range(2):
            u[:, k, 0:512] = uq[k, :, :, :64].reshape(P, 512)
            u[:, k, 512:768] = uq[k, :, :, 64:].reshape(P, 256)
        units.append(u.reshape(P, UW))
        ukv = a["w_ukv_2"][L].reshape(P, 8, 128)
        u = np.zeros((P, UW), f32)
        u[:, 0:512] = ukv[:, :, :64].reshape(P, 512)
        u[:, 512:1024] = ukv[:, :, 64:].reshape(P, 512)
        units.append(u)
        for b in (1, 2, 0):
            for j in range(4):
                units.append(iunit(w, r(2720 + 1024 * b + 256 * j)))
        for b in (1, 2, 0):
            for j in range(2):
                units.append(ounit(a["w_branch_2"][L, b], j))
        for j in range(4):
            units.append(ounit(a["w_out_2"][L], j))
        steps(lambda k: iunit(a["w_ffn_gate_2"][L], r(256 * k)), lambda k: iunit(a["w_ffn_up_2"][L], r(256 * k)),
              a["w_ffn_down_2"][L], FF_STEPS)
        units.append(ounit(a["w_ple_proj_2"][L], 0))
        for j in range(4):
            units.append(ounit(a["w_ple_gate_2"][L], j))
    W = np.stack(units)

    vat, vw = columns(VECS)
    vec = np.zeros((P, vw), f32)

    def put(name, cols):
        o, n = vat[name]
        vec[:, o:o + cols.shape[1]] = cols

    def tiles(v):
        return v.reshape(-1, P).T

    for L in range(2):
        put(f"norm_mix{L}", tiles(a["norm_mix"][L]))
        put(f"norm_ffn{L}", tiles(a["norm_ffn"][L]))
        cw = np.concatenate([a["ffn_conv_w"][L], a["ffn_conv_b"][L][None]]).reshape(4, 2, FF_STEPS, 2, P)
        put(f"cf{L}", cw.transpose(4, 2, 1, 3, 0).reshape(P, -1))
    put("pool_scale", tiles(a["pa_pool_scale"][0]))
    two = lambda g: np.concatenate([g, g])[:, None]
    four = lambda g: np.concatenate([g] * 4)[:, None]
    put("pa_gain", np.concatenate([two(a["pa_q_gain"][0])] * 4 + [two(a["pa_k_gain"][0])] * 4, 1))
    rgv = np.stack([*a["rg_conv_w"][0], a["rg_conv_b"][0], a["rg_b_a"][0], a["rg_b_x"][0], a["rg_lambda"][0]])
    put("rgv", rgv.reshape(8, RG_STEPS, 2, P).transpose(3, 1, 2, 0).reshape(P, -1))
    for L in range(2):
        for n, k in (("g_mix", "g_mix_2"), ("g_ffn", "g_ffn_2"), ("g_ple", "g_ple_2"), ("g_ple_in", "g_ple_in_2"),
                     ("g_cq", "g_q_lora_2"), ("g_ckv", "g_kv_lora_2"), ("g_dout", "g_diff_out_2")):
            put(f"{n}{L}", tiles(a[k][L]))
        put(f"g_diff{L}", np.concatenate([two(a["g_diff_q_2"][L])] * 4 + [two(a["g_diff_k_2"][L])] * 4, 1))
        put(f"g_win{L}", np.concatenate([two(a["g_win_q_2"][L])] * 4 + [two(a["g_win_k_2"][L])], 1))
        gq, gk = a["g_mla_q_2"][L], a["g_mla_k_2"][L]
        put(f"g_mla{L}", np.concatenate([two(gq[:64])] * 4 + [four(gq[64:])] * 2 + [two(gk[:64])] * 4, 1))
        put(f"g_krope{L}", four(gk[64:]))
        put(f"sink{L}", np.broadcast_to(a["win_sink_2"][L][None], (P, 8)))
        cw = np.concatenate([a["conv_w_2"][L], a["conv_b_2"][L][None]]).reshape(4, FF_STEPS, 2, P)
        put(f"cg{L}", cw.transpose(3, 1, 2, 0).reshape(P, -1))

    ra, rx = a["rg_w_a"][0], a["rg_w_x"][0]
    rw = np.stack([m for k in range(RG_STEPS) for m in (ra[2 * k], ra[2 * k + 1], rx[2 * k], rx[2 * k + 1])])
    lam = np.stack([np.stack([a[k][L] for k in ("lam_q1_2", "lam_k1_2", "lam_q2_2", "lam_k2_2")]) for L in range(2)])
    pos = a["positions_2"].reshape(S).astype(np.int32, copy=False)
    con, con0 = const_table()
    arrays = {
        "W": W,
        "XT": a["x"][0].T.reshape(DT, P, S).transpose(1, 0, 2),
        "CON": con,
        "CON0": con0,
        "VEC": vec,
        "PW": a["pa_pool_w"][0].transpose(1, 0, 2).reshape(P, 512),
        "RW": rw.transpose(1, 0, 2).reshape(P, 20 * P),
        "PE_T": a["p_2"][:, 0].transpose(0, 2, 1).reshape(2, 2, P, S).transpose(0, 2, 1, 3).reshape(2, P, 512),
        "POSR": pos.reshape(1, S),
        "POSC": pos.reshape(2, P).T,
        "LAM": lam.reshape(1, 512),
    }
    arrays = {k: np.ascontiguousarray(v) for k, v in arrays.items()}
    nc = bacc.Bacc("TRN2", target_bir_lowering=False, num_devices=1)
    args = [nc.dram_tensor(k, v.shape, mb.dt.from_np(v.dtype), kind="ExternalInput").ap() for k, v in arrays.items()]
    args.append(nc.dram_tensor("OUT", (P, DT, S), mb.dt.float32, kind="ExternalOutput").ap())
    build(nc, *args)
    out = run(nc, [arrays], core_ids=[0]).results[0]["OUT"]
    return np.ascontiguousarray(out.transpose(2, 1, 0).reshape(1, S, D))
```
